# Optimizing a Trainium2 kernel written in Bass

```python
import jax, jax.numpy as jnp
from jax import lax
import numpy as np
import math

D_MODEL = 1024
BATCH = 1
SEQ = 256
DEPTH = 4

N_MIXERS = 3
N_A = (DEPTH + 2) // 3
N_B = (DEPTH + 1) // 3
N_C = DEPTH // 3

N_HEADS = 16
HEAD_DIM = D_MODEL // N_HEADS
D_FF = ((8 * D_MODEL // 3 + 127) // 128) * 128
ROPE_THETA = 500000.0
ROT_DIM = HEAD_DIM // 4
Q_BLOCK = 128
EPS = 1e-6
NEG = -1e30

MOBA_BLOCK = 256
MOBA_TOPK = 3
MOBA_Q_CHUNK = 32

MLA_Q_RANK = 384
MLA_KV_RANK = 256
MLA_NOPE = 64
MLA_ROPE = 32
MLA_V = 64
MLA_IN = MLA_Q_RANK + MLA_KV_RANK + MLA_ROPE


def rms_norm(x, g):
    xf = x.astype(jnp.float32)
    y = xf * lax.rsqrt(jnp.mean(xf * xf, axis=-1, keepdims=True) + EPS)
    return (y * g.astype(jnp.float32)).astype(x.dtype)

def rotary(x, pos):
    r = x.shape[-1]
    inv = ROPE_THETA ** (-jnp.arange(0, r, 2, dtype=jnp.float32) / r)
    ang = pos.astype(jnp.float32)[:, None] * inv[None, :]
    cos, sin = jnp.cos(ang), jnp.sin(ang)
    xf = x.astype(jnp.float32)
    x1, x2 = xf[..., : r // 2], xf[..., r // 2:]
    return jnp.concatenate([x1 * cos - x2 * sin, x1 * sin + x2 * cos], axis=-1).astype(x.dtype)

def partial_rotary(x, pos):
    return jnp.concatenate([rotary(x[..., :ROT_DIM], pos), x[..., ROT_DIM:]], axis=-1)

def to_heads(t):
    b, s, _ = t.shape
    return t.reshape(b, s, N_HEADS, -1).transpose(0, 2, 1, 3)

def from_heads(t):
    b, h, s, d = t.shape
    return t.transpose(0, 2, 1, 3).reshape(b, s, h * d)

def merge_blocks(o):
    nb, b, h, q, d = o.shape
    return o.transpose(1, 2, 0, 3, 4).reshape(b, h, nb * q, d)

def swiglu(x, w_gate_up, w_down):
    g, u = jnp.split(x @ w_gate_up, 2, axis=-1)
    return (jax.nn.silu(g) * u) @ w_down

def stick_breaking_attention(x, w_qkv, w_o):
    b, s, _ = x.shape
    q, k, v = (to_heads(t) for t in jnp.split(x @ w_qkv, 3, axis=-1))
    scale = HEAD_DIM ** -0.5
    kpos = jnp.arange(s)

    def block(i):
        q0 = i * Q_BLOCK
        qb = lax.dynamic_slice_in_dim(q, q0, Q_BLOCK, axis=2)
        z = jnp.einsum('bhqd,bhkd->bhqk', qb, k).astype(jnp.float32) * scale
        qpos = q0 + jnp.arange(Q_BLOCK)
        past = kpos[None, :] < qpos[:, None]
        log_keep = jnp.where(past, -jax.nn.softplus(z), 0.0)
        tail = lax.cumsum(log_keep, axis=3, reverse=True) - log_keep
        w = jnp.where(past, jnp.exp(jax.nn.log_sigmoid(z) + tail), 0.0)
        return jnp.einsum('bhqk,bhkd->bhqd', w.astype(v.dtype), v)

    o = merge_blocks(lax.map(block, jnp.arange(s // Q_BLOCK)))
    return from_heads(o) @ w_o

def moba_attention(x, w_qkv, w_o):
    b, s, _ = x.shape
    pos = jnp.arange(s)
    q, k, v = (to_heads(t) for t in jnp.split(x @ w_qkv, 3, axis=-1))
    q, k = partial_rotary(q, pos), partial_rotary(k, pos)
    nb = -(-s // MOBA_BLOCK)
    s_pad = nb * MOBA_BLOCK
    pad = [(0, 0), (0, 0), (0, s_pad - s), (0, 0)]
    q, k, v = jnp.pad(q, pad), jnp.pad(k, pad), jnp.pad(v, pad)
    kb = k.reshape(b, N_HEADS, nb, MOBA_BLOCK, HEAD_DIM)
    vb = v.reshape(b, N_HEADS, nb, MOBA_BLOCK, HEAD_DIM)
    scale = HEAD_DIM ** -0.5

    k_mean = jnp.mean(kb.astype(jnp.float32), axis=3)
    gate = jnp.einsum('bhsd,bhnd->bhsn', q.astype(jnp.float32), k_mean)
    q_blk = jnp.arange(s_pad) // MOBA_BLOCK
    past_blk = jnp.arange(nb)[None, :] < q_blk[:, None]
    gate = jnp.where(past_blk, gate, NEG)
    topk = min(MOBA_TOPK, nb)
    _, sel = lax.top_k(gate, topk)
    sel_valid = sel < q_blk[:, None]

    bi = jnp.arange(b)[:, None, None, None]
    hi = jnp.arange(N_HEADS)[None, :, None, None]

    def chunk(c):
        q0 = c * MOBA_Q_CHUNK
        qc = lax.dynamic_slice_in_dim(q, q0, MOBA_Q_CHUNK, axis=2)
        idx = lax.dynamic_slice_in_dim(sel, q0, MOBA_Q_CHUNK, axis=2)
        valid = lax.dynamic_slice_in_dim(sel_valid, q0, MOBA_Q_CHUNK, axis=2)
        kg = kb[bi, hi, idx]
        vg = vb[bi, hi, idx]
        l_sel = jnp.einsum('bhqd,bhqjkd->bhqjk', qc, kg).astype(jnp.float32) * scale
        l_sel = jnp.where(valid[..., None], l_sel, NEG)
        l_sel = l_sel.reshape(b, N_HEADS, MOBA_Q_CHUNK, topk * MOBA_BLOCK)
        own = q0 // MOBA_BLOCK
        k_own = lax.dynamic_index_in_dim(kb, own, axis=2, keepdims=False)
        v_own = lax.dynamic_index_in_dim(vb, own, axis=2, keepdims=False)
        l_own = jnp.einsum('bhqd,bhkd->bhqk', qc, k_own).astype(jnp.float32) * scale
        cpos = q0 + jnp.arange(MOBA_Q_CHUNK)
        opos = own * MOBA_BLOCK + jnp.arange(MOBA_BLOCK)
        l_own = jnp.where(opos[None, :] <= cpos[:, None], l_own, NEG)
        p = jax.nn.softmax(jnp.concatenate([l_sel, l_own], axis=-1), axis=-1).astype(v.dtype)
        p_sel = p[..., : topk * MOBA_BLOCK].reshape(b, N_HEADS, MOBA_Q_CHUNK, topk, MOBA_BLOCK)
        p_own = p[..., topk * MOBA_BLOCK:]
        return (jnp.einsum('bhqjk,bhqjkd->bhqd', p_sel, vg)
                + jnp.einsum('bhqk,bhkd->bhqd', p_own, v_own))

    o = merge_blocks(lax.map(chunk, jnp.arange(s_pad // MOBA_Q_CHUNK)))[:, :, :s]
    return from_heads(o) @ w_o

def mla_attention(x, w_in, q_norm, w_uq, kv_norm, w_ukv, w_o):
    b, s, _ = x.shape
    pos = jnp.arange(s)
    cq, ckv, kr = jnp.split(x @ w_in, [MLA_Q_RANK, MLA_Q_RANK + MLA_KV_RANK], axis=-1)
    q = to_heads(rms_norm(cq, q_norm) @ w_uq)
    q_nope, q_rope = q[..., :MLA_NOPE], rotary(q[..., MLA_NOPE:], pos)
    kv = to_heads(rms_norm(ckv, kv_norm) @ w_ukv)
    k_nope, v = kv[..., :MLA_NOPE], kv[..., MLA_NOPE:]
    k_rope = rotary(kr, pos)
    scale = (MLA_NOPE + MLA_ROPE) ** -0.5
    kpos = jnp.arange(s)

    def block(i):
        q0 = i * Q_BLOCK
        qn = lax.dynamic_slice_in_dim(q_nope, q0, Q_BLOCK, axis=2)
        qr = lax.dynamic_slice_in_dim(q_rope, q0, Q_BLOCK, axis=2)
        logits = (jnp.einsum('bhqd,bhkd->bhqk', qn, k_nope)
                  + jnp.einsum('bhqr,bkr->bhqk', qr, k_rope)).astype(jnp.float32) * scale
        qpos = q0 + jnp.arange(Q_BLOCK)
        logits = jnp.where(kpos[None, :] <= qpos[:, None], logits, NEG)
        p = jax.nn.softmax(logits, axis=-1).astype(v.dtype)
        return jnp.einsum('bhqk,bhkd->bhqd', p, v)

    o = merge_blocks(lax.map(block, jnp.arange(s // Q_BLOCK)))
    return from_heads(o) @ w_o

def first_inputs(seed: int = 0) -> dict:
    key = jax.random.key(seed)
    ks = iter(jax.random.split(key, 32))

    def w(shape, fan_in):
        return jax.random.normal(next(ks), shape, jnp.float32) * (fan_in ** -0.5)

    def gain(shape):
        return 1.0 + 0.02 * jax.random.normal(next(ks), shape, jnp.float32)

    D = D_MODEL
    return {
        "x": jax.random.normal(next(ks), (BATCH, SEQ, D), jnp.float32),
        "norm_ffn1": gain((DEPTH, D)),
        "ffn1_w_gate_up": w((DEPTH, D, 2 * D_FF), D),
        "ffn1_w_down": w((DEPTH, D_FF, D), D_FF),
        "norm_mix": gain((DEPTH, D)),
        "norm_ffn2": gain((DEPTH, D)),
        "ffn2_w_gate_up": w((DEPTH, D, 2 * D_FF), D),
        "ffn2_w_down": w((DEPTH, D_FF, D), D_FF),
        "sb_w_qkv": w((N_A, D, 3 * D), D),
        "sb_w_o": w((N_A, D, D), D),
        "moba_w_qkv": w((N_B, D, 3 * D), D),
        "moba_w_o": w((N_B, D, D), D),
        "mla_w_in": w((N_C, D, MLA_IN), D),
        "mla_q_norm": gain((N_C, MLA_Q_RANK)),
        "mla_w_uq": w((N_C, MLA_Q_RANK, N_HEADS * (MLA_NOPE + MLA_ROPE)), MLA_Q_RANK),
        "mla_kv_norm": gain((N_C, MLA_KV_RANK)),
        "mla_w_ukv": w((N_C, MLA_KV_RANK, N_HEADS * (MLA_NOPE + MLA_V)), MLA_KV_RANK),
        "mla_w_o": w((N_C, N_HEADS * MLA_V, D), N_HEADS * MLA_V),
        "final_norm": gain((D,)),
    }

def first_block(x, norm_ffn1, ffn1_w_gate_up, ffn1_w_down, norm_mix, norm_ffn2,
              ffn2_w_gate_up, ffn2_w_down, sb_w_qkv, sb_w_o, moba_w_qkv, moba_w_o,
              mla_w_in, mla_q_norm, mla_w_uq, mla_kv_norm, mla_w_ukv, mla_w_o,
              final_norm):
    h = x
    for i in range(DEPTH):
        h = h + 0.5 * swiglu(rms_norm(h, norm_ffn1[i]), ffn1_w_gate_up[i], ffn1_w_down[i])
        hn = rms_norm(h, norm_mix[i])
        kind, j = i % N_MIXERS, i // N_MIXERS
        if kind == 0:
            mix = stick_breaking_attention(hn, sb_w_qkv[j], sb_w_o[j])
        elif kind == 1:
            mix = moba_attention(hn, moba_w_qkv[j], moba_w_o[j])
        else:
            mix = mla_attention(hn, mla_w_in[j], mla_q_norm[j], mla_w_uq[j],
                                mla_kv_norm[j], mla_w_ukv[j], mla_w_o[j])
        h = h + mix
        h = h + 0.5 * swiglu(rms_norm(h, norm_ffn2[i]), ffn2_w_gate_up[i], ffn2_w_down[i])
    return rms_norm(h, final_norm)


DEPTH_2 = 2

HEAD_DIM_2 = 64
DA_HEADS = 4
DA_QK = HEAD_DIM_2
DA_V = 2 * HEAD_DIM_2
DA_WIDTH = DA_HEADS * DA_V
ROT_DIM_2 = HEAD_DIM_2 // 4
SC_WIDTH = 256
SC_GROUPS = 4
CONV_W = 3
GLA_HEADS = 4
GLA_DK = 32
GLA_DV = 64
GLA_KW = GLA_HEADS * GLA_DK
GLA_VW = GLA_HEADS * GLA_DV
GLA_GATE_RANK = 16
GLA_GATE_TEMP = 16.0
GLA_CHUNK = 64
MIX_WIDTH = DA_WIDTH + SC_WIDTH + GLA_VW
IN_SIZES = (DA_HEADS * 2 * DA_QK, DA_HEADS * 2 * DA_QK, DA_WIDTH,
            SC_WIDTH, SC_WIDTH, SC_WIDTH,
            GLA_KW, GLA_KW, GLA_VW, GLA_VW, GLA_GATE_RANK)
IN_WIDTH = 3088
PEER_HEADS = 8
PEER_NKEYS = 128
PEER_EXPERTS = PEER_NKEYS * PEER_NKEYS
PEER_HALF = 128
PEER_QDIM = 2 * PEER_HALF
PEER_TOPK = 16
PEER_TOKEN_BLOCK = 128


def rmsnorm(x, g):
    xf = x.astype(jnp.float32)
    y = xf * lax.rsqrt(jnp.mean(xf * xf, axis=-1, keepdims=True) + EPS)
    return (y * g.astype(jnp.float32)).astype(x.dtype)

def rope_tables(positions):
    inv = ROPE_THETA ** (-jnp.arange(0, ROT_DIM_2, 2, dtype=jnp.float32) / ROT_DIM_2)
    ang = positions.astype(jnp.float32)[..., None] * inv
    return jnp.cos(ang), jnp.sin(ang)

def apply_partial_rope(t, cos, sin):
    rot, rest = t[..., :ROT_DIM_2], t[..., ROT_DIM_2:]
    r1, r2 = rot[..., :ROT_DIM_2 // 2], rot[..., ROT_DIM_2 // 2:]
    c = cos[:, :, None, None, :].astype(t.dtype)
    s = sin[:, :, None, None, :].astype(t.dtype)
    return jnp.concatenate([r1 * c - r2 * s, r1 * s + r2 * c, rest], axis=-1)

def diff_attention(q, k, v, lam, out_scale, gain):
    B, S = q.shape[0], q.shape[1]
    nblk = S // Q_BLOCK
    qb = q.reshape(B, nblk, Q_BLOCK, DA_HEADS, 2, DA_QK).transpose(1, 0, 2, 3, 4, 5)
    kpos = jnp.arange(S)
    scale = DA_QK ** -0.5

    def block(args):
        qi, bi = args
        s = jnp.einsum('bqhmd,bkhmd->bhmqk', qi, k).astype(jnp.float32) * scale
        qpos = bi * Q_BLOCK + jnp.arange(Q_BLOCK)
        mask = kpos[None, :] <= qpos[:, None]
        p = jax.nn.softmax(jnp.where(mask, s, -jnp.inf), axis=-1)
        a = p[:, :, 0] - lam * p[:, :, 1]
        return jnp.einsum('bhqk,bkhe->bqhe', a.astype(v.dtype), v)

    o = lax.map(block, (qb, jnp.arange(nblk)))
    o = o.transpose(1, 0, 2, 3, 4).reshape(B, S, DA_HEADS, DA_V)
    o = rmsnorm(o, gain) * out_scale
    return o.reshape(B, S, DA_WIDTH)

def short_conv(b_gate, c_gate, h_in, w):
    z = c_gate * h_in
    S = z.shape[1]
    zp = jnp.pad(z, ((0, 0), (CONV_W - 1, 0), (0, 0)))
    y = w[0] * zp[:, 0:S]
    for j in range(1, CONV_W):
        y = y + w[j] * zp[:, j:j + S]
    return b_gate * y

def gla(q, k, v, log_a):
    B, S = q.shape[0], q.shape[1]
    nc = S // GLA_CHUNK

    def chunks(t):
        return t.astype(jnp.float32).reshape(B, nc, GLA_CHUNK, GLA_HEADS, t.shape[-1]).transpose(1, 0, 3, 2, 4)

    qc, kc, vc, ac = chunks(q * (GLA_DK ** -0.5)), chunks(k), chunks(v), chunks(log_a)
    causal = jnp.tril(jnp.ones((GLA_CHUNK, GLA_CHUNK), dtype=bool))

    def step(state, inp):
        qi, ki, vi, ai = inp
        b = lax.cumsum(ai, axis=2)
        diff = b[:, :, :, None, :] - b[:, :, None, :, :]
        decay = jnp.exp(jnp.where(causal[:, :, None], diff, -jnp.inf))
        attn = jnp.sum(qi[:, :, :, None, :] * ki[:, :, None, :, :] * decay, axis=-1)
        o = jnp.einsum('bhij,bhje->bhie', attn, vi) + jnp.einsum('bhid,bhde->bhie', qi * jnp.exp(b), state)
        b_last = b[:, :, -1:, :]
        state = jnp.exp(b_last[:, :, 0, :, None]) * state + jnp.einsum(
            'bhjd,bhje->bhde', ki * jnp.exp(b_last - b), vi)
        return state, o

    state0 = jnp.zeros((B, GLA_HEADS, GLA_DK, GLA_DV), jnp.float32)
    _, o = lax.scan(step, state0, (qc, kc, vc, ac))
    o = o.transpose(1, 0, 3, 2, 4).reshape(B, S, GLA_HEADS, GLA_DV)
    return o.astype(v.dtype)

def peer(xn, w_q, keys1, keys2, u, v):
    B, S, D = xn.shape
    T = B * S
    xt = xn.reshape(T, D)
    q = (xt @ w_q).reshape(T, PEER_HEADS, 2, PEER_HALF)
    s1 = jnp.einsum('thd,nd->thn', q[:, :, 0], keys1).astype(jnp.float32)
    s2 = jnp.einsum('thd,nd->thn', q[:, :, 1], keys2).astype(jnp.float32)
    v1, i1 = lax.top_k(s1, PEER_TOPK)
    v2, i2 = lax.top_k(s2, PEER_TOPK)
    cand = (v1[..., :, None] + v2[..., None, :]).reshape(T, PEER_HEADS, PEER_TOPK * PEER_TOPK)
    sc, ci = lax.top_k(cand, PEER_TOPK)
    e1 = jnp.take_along_axis(i1, ci // PEER_TOPK, axis=-1)
    e2 = jnp.take_along_axis(i2, ci % PEER_TOPK, axis=-1)
    hk = PEER_HEADS * PEER_TOPK
    experts = (e1 * PEER_NKEYS + e2).reshape(T, hk)
    gates = jax.nn.softmax(sc, axis=-1).reshape(T, hk).astype(xn.dtype)
    nb = T // PEER_TOKEN_BLOCK

    def block(args):
        xb, eb, gb = args
        ub = jnp.take(u, eb, axis=0)
        hb = jax.nn.gelu(jnp.einsum('tkd,td->tk', ub, xb), approximate=False)
        vb = jnp.take(v, eb, axis=0)
        return jnp.einsum('tk,tkd->td', gb * hb, vb)

    out = lax.map(block, (xt.reshape(nb, PEER_TOKEN_BLOCK, D),
                          experts.reshape(nb, PEER_TOKEN_BLOCK, hk),
                          gates.reshape(nb, PEER_TOKEN_BLOCK, hk)))
    return out.reshape(B, S, D)

def second_inputs(seed: int = 0) -> dict:
    key = jax.random.key(seed)
    ks = jax.random.split(key, 24)
    f32 = jnp.float32
    L, D = DEPTH_2, D_MODEL
    nrm = lambda k, shape, s: jax.random.normal(k, shape, f32) * s
    return {
        "x": jax.random.normal(ks[0], (BATCH, SEQ, D), f32),
        "positions": jnp.broadcast_to(jnp.arange(SEQ, dtype=jnp.int32), (BATCH, SEQ)),
        "norm_mix": 1.0 + nrm(ks[1], (L, D), 0.02),
        "w_in": nrm(ks[2], (L, D, IN_WIDTH), D ** -0.5),
        "lam_q1": nrm(ks[3], (L, DA_QK), 0.1),
        "lam_k1": nrm(ks[4], (L, DA_QK), 0.1),
        "lam_q2": nrm(ks[5], (L, DA_QK), 0.1),
        "lam_k2": nrm(ks[6], (L, DA_QK), 0.1),
        "diff_norm": 1.0 + nrm(ks[7], (L, DA_V), 0.02),
        "conv_w": nrm(ks[8], (L, CONV_W, SC_WIDTH), CONV_W ** -0.5),
        "gla_w_gate2": nrm(ks[9], (L, GLA_GATE_RANK, GLA_KW), GLA_GATE_RANK ** -0.5),
        "gla_b_gate": nrm(ks[10], (L, GLA_KW), 0.1),
        "gla_norm": 1.0 + nrm(ks[11], (L, GLA_DV), 0.02),
        "w_out": nrm(ks[12], (L, MIX_WIDTH, D), MIX_WIDTH ** -0.5),
        "norm_ffn": 1.0 + nrm(ks[13], (L, D), 0.02),
        "peer_w_q": nrm(ks[14], (L, D, PEER_HEADS * PEER_QDIM), D ** -0.5),
        "peer_keys1": nrm(ks[15], (L, PEER_NKEYS, PEER_HALF), PEER_HALF ** -0.5),
        "peer_keys2": nrm(ks[16], (L, PEER_NKEYS, PEER_HALF), PEER_HALF ** -0.5),
        "peer_u": nrm(ks[17], (L, PEER_EXPERTS, D), D ** -0.5),
        "peer_v": nrm(ks[18], (L, PEER_EXPERTS, D), (PEER_HEADS * PEER_TOPK) ** -0.5),
        "norm_final": 1.0 + nrm(ks[19], (D,), 0.02),
    }

def second_block(x, positions, norm_mix, w_in, lam_q1, lam_k1, lam_q2, lam_k2, diff_norm,
              conv_w, gla_w_gate2, gla_b_gate, gla_norm, w_out, norm_ffn, peer_w_q,
              peer_keys1, peer_keys2, peer_u, peer_v, norm_final):
    B, S, _ = x.shape
    cos, sin = rope_tables(positions)
    split_points = [int(p) for p in np.cumsum(IN_SIZES)[:-1]]
    for i in range(DEPTH_2):
        h = rmsnorm(x, norm_mix[i])
        proj = h @ w_in[i]
        (da_q, da_k, da_v, sc_b, sc_c, sc_h,
         g_q, g_k, g_v, g_r, g_lr) = jnp.split(proj, split_points, axis=-1)

        lam_init = 0.8 - 0.6 * math.exp(-0.3 * i)
        lam = (jnp.exp(jnp.sum(lam_q1[i].astype(jnp.float32) * lam_k1[i].astype(jnp.float32)))
               - jnp.exp(jnp.sum(lam_q2[i].astype(jnp.float32) * lam_k2[i].astype(jnp.float32)))
               + lam_init)
        q = apply_partial_rope(da_q.reshape(B, S, DA_HEADS, 2, DA_QK), cos, sin)
        k = apply_partial_rope(da_k.reshape(B, S, DA_HEADS, 2, DA_QK), cos, sin)
        o_da = diff_attention(q, k, da_v.reshape(B, S, DA_HEADS, DA_V), lam,
                              1.0 - lam_init, diff_norm[i])

        o_sc = short_conv(sc_b, sc_c, sc_h, conv_w[i])

        log_a = jax.nn.log_sigmoid((g_lr @ gla_w_gate2[i] + gla_b_gate[i]).astype(jnp.float32)) / GLA_GATE_TEMP
        o_g = gla(g_q.reshape(B, S, GLA_HEADS, GLA_DK), g_k.reshape(B, S, GLA_HEADS, GLA_DK),
                  g_v.reshape(B, S, GLA_HEADS, GLA_DV), log_a.reshape(B, S, GLA_HEADS, GLA_DK))
        o_g = rmsnorm(o_g, gla_norm[i]) * jax.nn.silu(g_r.reshape(B, S, GLA_HEADS, GLA_DV))
        o_g = o_g.reshape(B, S, GLA_VW)

        mixed = jnp.concatenate([o_da, o_sc, o_g], axis=-1)
        x = x + mixed @ w_out[i]

        x = x + peer(rmsnorm(x, norm_ffn[i]), peer_w_q[i], peer_keys1[i], peer_keys2[i],
                     peer_u[i], peer_v[i])
    return rmsnorm(x, norm_final)


def setup_inputs(seed=0):
    out = dict(first_inputs(seed))
    for name, value in second_inputs(seed + 1).items():
        if name != "x":
            out[name + "_2"] = value
    return out


def reference(
    x, norm_ffn1, ffn1_w_gate_up, ffn1_w_down, norm_mix, norm_ffn2, ffn2_w_gate_up, ffn2_w_down,
    sb_w_qkv, sb_w_o, moba_w_qkv, moba_w_o, mla_w_in, mla_q_norm, mla_w_uq, mla_kv_norm,
    mla_w_ukv, mla_w_o, final_norm, positions_2, norm_mix_2, w_in_2, lam_q1_2, lam_k1_2,
    lam_q2_2, lam_k2_2, diff_norm_2, conv_w_2, gla_w_gate2_2, gla_b_gate_2, gla_norm_2, w_out_2,
    norm_ffn_2, peer_w_q_2, peer_keys1_2, peer_keys2_2, peer_u_2, peer_v_2, norm_final_2,
):
    x = first_block(
        x, norm_ffn1, ffn1_w_gate_up, ffn1_w_down, norm_mix, norm_ffn2, ffn2_w_gate_up,
        ffn2_w_down, sb_w_qkv, sb_w_o, moba_w_qkv, moba_w_o, mla_w_in, mla_q_norm, mla_w_uq,
        mla_kv_norm, mla_w_ukv, mla_w_o, final_norm,
    )
    return second_block(
        x, positions_2, norm_mix_2, w_in_2, lam_q1_2, lam_k1_2, lam_q2_2, lam_k2_2, diff_norm_2,
        conv_w_2, gla_w_gate2_2, gla_b_gate_2, gla_norm_2, w_out_2, norm_ffn_2, peer_w_q_2,
        peer_keys1_2, peer_keys2_2, peer_u_2, peer_v_2, norm_final_2,
    )


_drawn_inputs = setup_inputs


def setup_inputs(seed=0):
    import zlib

    import numpy as np

    out = dict(_drawn_inputs(seed))
    spreads = {}
    factors = {'mla_q_norm': 8.0,
     'mla_kv_norm': 5.017,
     'diff_norm_2': 4.348,
     'gla_b_gate_2': 2.971,
     'gla_norm_2': 6.99,
     'norm_ffn_2': 7.541}
    for name, (base, spread) in spreads.items():
        noise = np.random.default_rng([zlib.crc32(name.encode()), seed]).standard_normal(out[name].shape)
        drawn = base * np.exp(spread * noise) if base else spread * noise
        out[name] = __import__('jax').numpy.asarray(drawn.astype(out[name].dtype))
    for name, factor in factors.items():
        out[name] = (out[name] * factor).astype(out[name].dtype)
    return out
```

```python
import math
from contextlib import ExitStack

import numpy as np

import concourse.bass as bass
from concourse import mybir

F32 = mybir.dt.float32
U32 = mybir.dt.uint32
I32 = mybir.dt.int32
ALU = mybir.AluOpType
ACT = mybir.ActivationFunctionType
AX = mybir.AxisListType.X

P = 128
D = 1024
TOK = 256
TT = TOK // P
KT = D // P
HEADS = 16
HD = D // HEADS
DEPTH, DEPTH2 = 4, 2
D_FF = ((8 * D // 3 + 127) // 128) * 128
FFN_STEP = 256
FFN_STEPS = D_FF // FFN_STEP
EPS = 1e-6
NEG = -1e30
THETA = 500000.0
TRI = 384

Q_RANK, KV_RANK, ROPE = 384, 256, 32
MLA_IN = Q_RANK + KV_RANK + ROPE
MLA_QK = 64 + ROPE

DA_HEADS, DA_V = 4, 128
GLA_HEADS, GLA_DK, GLA_DV, GLA_RANK = 4, 32, 64, 16
GLA_TEMP = 16.0
SUB = 16
NSUB = P // SUB
IN_WIDTH = 3088

PK_HEADS, NKEYS, TOPK = 8, 128, 16
EXPERTS = NKEYS * NKEYS
PICKS = PK_HEADS * TOPK

GSLOTS, GCOLS = 4, 512
DSLOTS, DROWS = 2, 256
ROWSLOTS = GSLOTS * KT * GCOLS // D
BURST = 16

FREQS = [16, ROPE, 16]
FREQ_AT = [0, 8, 24]
NFREQ = 32


class Phase:

    def __init__(self, kind, i=None, j=None, which=None, gain=None, last=None):
        self.kind, self.i, self.j, self.which, self.gain, self.last = kind, i, j, which, gain, last


def panels_of(kind):
    if kind == "sb":
        return [(512 * i, 512, "T" if i < 4 else "rows") for i in range(6)]
    if kind == "moba":
        return [(512 * i, 512, "rows") for i in range(6)]
    if kind == "mla_in":
        return [(0, 512, "rows"), (512, MLA_IN - 512, "rows")]
    if kind == "mla_uq":
        return [(512 * i, 512, "rows") for i in range(3)]
    if kind == "mla_ukv":
        return [(512 * i, 512, "rows") for i in range(4)]
    if kind == "pq":
        return [(512 * i, 512, "T") for i in range(4)]
    return [(0, 512, "rows"), (512, 512, "rows"), (1024, 512, "rows"), (1536, 512, "T"),
            (2048, 512, "T"), (2560, 512, "rows"), (3072, GLA_RANK, "narrow")]


RAISES = {
    "norm": dict(square_sum=2, mean_square=1, rstd=1, normed=2, turned=4, turned_act=2,
                 turned_dve=2, gains=1),
    "norm_final": dict(square_sum=2, mean_square=1, rstd=1, normed=2, gains=1),
    "ffn": dict(wide=2 * FFN_STEPS, wide_read=2 * FFN_STEPS, silu=2 * FFN_STEPS,
                deep=FFN_STEPS, resid=4),
    "sb": dict(wide=12, wide_read=12, deep=4, resid=4, scores=HEADS, masked=HEADS, log1p=HEADS,
               softplus=HEADS, tail=HEADS, tail_read=HEADS, weights=HEADS, mixed=HEADS,
               mixed_read=HEADS),
    "moba": dict(wide=12, wide_read=12, deep=4, resid=4, rotated=1, turned=8, turned_act=4,
                 turned_dve=4, scores=HEADS, masked=HEADS, row_max=HEADS, exps=HEADS,
                 probs=HEADS, probs_T=HEADS, weights=HEADS, mixed=HEADS, mixed_read=HEADS),
    "mla": dict(wide=18, wide_read=18, deep=4, resid=4, rotated=3, mean_square=1, rstd=1,
                turned=20, turned_act=10, turned_dve=10,
                scores=HEADS, masked=HEADS, row_max=HEADS, exps=HEADS,
                probs=HEADS, probs_T=HEADS, weights=HEADS, mixed=HEADS, mixed_read=HEADS),
    "mix2": dict(wide=14, wide_read=14, deep=4, resid=4, rotated=2, mean_square=2, rstd=2,
                 turned=8, turned_act=4, turned_dve=4,
                 scores=8, masked=8, row_max=8, exps=8, probs=8, probs_T=4, weights=4,
                 mixed=4, mixed_read=4),
    "peer": dict(wide=8, wide_read=8, turned=2, turned_act=1, turned_dve=1, key_scores=8,
                 key_scores_read=8, row_used=4 * PICKS),
}


def plan():
    phases = []
    for i in range(DEPTH):
        phases += [Phase("norm", gain=("norm_ffn1", i)), Phase("ffn", which=1, i=i),
                   Phase("norm", gain=("norm_mix", i)),
                   Phase(("sb", "moba", "mla")[i % 3], i=i, j=i // 3),
                   Phase("norm", gain=("norm_ffn2", i)), Phase("ffn", which=2, i=i)]
    phases.append(Phase("norm_final", gain=("final_norm", None), last=False))
    for i in range(DEPTH2):
        phases += [Phase("norm", gain=("norm_mix_2", i)), Phase("mix2", i=i),
                   Phase("norm", gain=("norm_ffn_2", i)), Phase("peer", i=i)]
    phases.append(Phase("norm_final", gain=("norm_final_2", None), last=True))
    total = {}
    for n, ph in enumerate(phases):
        ph.n = n
        ph.at = dict(total)
        for name, count in RAISES[ph.kind].items():
            total[name] = total.get(name, 0) + count
    return phases


def build(nc, A, out, stop=None):
    phases = plan()[:stop]
    ctx = ExitStack()
    with ctx:
        def sb(name, shape, dt=F32):
            return ctx.enter_context(nc.sbuf_tensor(name, shape, dt))

        def sem(name):
            return ctx.enter_context(nc.semaphore(name))

        wide_ring = sb("wide_ring", [P, GSLOTS, KT, GCOLS])
        deep_ring = sb("deep_ring", [P, DSLOTS, DROWS // P, D])
        row_ring = wide_ring[:].rearrange("p a b c -> p (a b c)").rearrange("p (n d) -> p n d", d=D)
        resid = sb("resid", [P, TT, D])
        xn = sb("xn", [P, TT, D])
        xT = sb("xT", [P, KT, TOK])
        gains = sb("gains", [P, 2, D])
        arena = sb("arena", [P, 18432])

        def cut(at, *shape):
            n = int(np.prod(shape))
            assert at + n <= 18432, (at, shape)
            v = arena[:, at:at + n]
            names = " ".join("abcd"[:len(shape)])
            if len(shape) == 1:
                return v
            return v.rearrange(f"p ({names}) -> p {names}",
                               **{x: s for x, s in zip("abcd", shape)})

        hidden = cut(0, 4, TOK)
        silu_buf = cut(1024, 2, TOK)
        CORE = 16128
        core_a = cut(CORE, 2, TRI)
        core_b = cut(CORE + 768, 2, TRI)
        core_c = cut(CORE + 1536, 2, TRI)
        core_d = cut(CORE - 768, 2, TRI)
        core_e = cut(CORE - 1536, 2, TRI)
        sb_qT, sb_kT = cut(0, KT, TOK), cut(2048, KT, TOK)
        sb_v = cut(4096, TT, D)
        oT = cut(6144, KT, TOK)
        mo_qk = cut(8192, TT, 2 * D)
        mo_T = cut(0, 2 * KT, TOK)
        mo_v = cut(4096, TT, D)
        ml_T = cut(0, HEADS, 4 * P)
        ml_v = cut(8192, TT, D)
        ml_q = cut(10240, TT, HEADS, MLA_QK)
        ml_k = cut(13312, TT, HEADS, MLA_QK)
        ml_c = cut(16384, TT, MLA_IN)
        ml_oT = cut(10240, KT, TOK)
        ml_cT = xT[:, 0:5, :]
        m2_qk = cut(0, TT, 1024)
        m2_v = cut(2048, TT, DA_HEADS * DA_V)
        m2_sc = cut(3072, 6, TOK)
        m2_gq = cut(4608, 2, TOK)
        m2_gv = cut(5120, TT, 512)
        m2_lr = cut(6144, TOK)
        m2_b = cut(6400, TOK)
        m2_la = cut(6656, 3, TOK)
        m2_diag = cut(7424, 2, SUB, NSUB, SUB)
        m2_qkT = cut(7424, KT, TOK)
        m2_AT = cut(11520, 3, GLA_HEADS, P)
        m2_og = cut(13056, TT, 256)
        m2_od = cut(13568, TT, 512)
        m2_tmp = cut(14592, 2, 512)
        m2_mixT = xT
        m2_qsb = xn[:, 0, :].rearrange("p (n h i) -> p n h i", h=GLA_HEADS, i=SUB)
        m2_ks = xn[:, 1, :].rearrange("p (n t) -> p n t", t=TOK)
        pk_S = cut(0, TT, 16, NKEYS)
        pk_qT = cut(4096, 16, TOK)
        pk_cand = cut(8192, 256)
        pk_v = cut(8448, 16, TOPK)
        pk_i = cut(8704, 16, TOPK).bitcast(U32)
        pk_if = cut(8960, 16, TOPK)
        pk_hot = cut(9216, PK_HEADS * TOPK, TOPK)
        pk_sc = cut(11264, PK_HEADS, TOPK)
        pk_ci = cut(11392, PK_HEADS, TOPK).bitcast(U32)
        pk_ab = cut(11520, 2, PICKS)
        pk_abu = cut(11776, 2, PICKS).bitcast(U32)
        pk_e = cut(12032, 2, PICKS)
        pk_gate = cut(12288, TT, PICKS)
        pk_dot = cut(12544, PICKS)
        pk_coef = cut(12672, PICKS)
        pk_idx = cut(12800, TT, PICKS).bitcast(U32)
        pk_burst = cut(13056, 2, BURST).bitcast(U32)
        pk_dots = cut(13088, 2, BURST)
        pk_den = cut(13120, PK_HEADS)
        pk_scratch = cut(13312, D)
        pk_keys = cut(14336, 2, PEER_D := P)
        pk_keysT = cut(14592, 2, P)

        ident = sb("ident", [P, P])
        ones = sb("ones", [P, P])
        later = sb("later", [P, P])
        mask_T = sb("mask_T", [P, TRI])
        mask_rows = sb("mask_rows", [P, TRI])
        head_of = sb("head_of", [P, GLA_HEADS])
        earlier_sub = sb("earlier_sub", [P, NSUB])
        same_sub = sb("same_sub", [P, NSUB, SUB])
        iota16 = sb("iota16", [P, TOPK])
        minus_half = sb("minus_half", [P, 16])
        zeros_tok = sb("zeros_tok", [P, TOK])
        trig = sb("trig", [P, 2, TT, NFREQ])
        ang = sb("ang", [P, 4, TT, NFREQ])
        inv_freq = sb("inv_freq", [P, NFREQ])
        posf = sb("posf", [P, 2, TT])
        posi = sb("posi", [P, TT], I32)
        small = sb("small", [P, 64])
        mla_gain = sb("mla_gain", [P, Q_RANK + KV_RANK])
        diff_gain = sb("diff_gain", [P, DEPTH2, DA_V])
        gla_gain = sb("gla_gain", [P, DEPTH2, GLA_DV])
        lam_rows = sb("lam_rows", [P, DEPTH2, 4, 64])
        minus_lam = sb("minus_lam", [P, DEPTH2])
        conv_taps = sb("conv_taps", [P, DEPTH2, 2, 3])
        gate2 = sb("gate2", [GLA_RANK, DEPTH2, P])
        gate_bias = sb("gate_bias", [P, DEPTH2])

        bank = [ctx.enter_context(nc.psum_tensor(f"bank{i}", [P, 512], F32)) for i in range(8)]
        acc = [[bank[0], bank[1]], [bank[2], bank[3]]]
        work = bank[4:8]

        S = {name: sem(name) for name in (
            "square_sum",
            "mean_square",
            "rstd",
            "normed",
            "turned",
            "turned_act",
            "turned_dve",
            "wide",
            "wide_read",
            "silu",
            "deep",
            "resid",
            "scores",
            "masked",
            "log1p",
            "softplus",
            "tail",
            "tail_read",
            "row_max",
            "exps",
            "probs",
            "probs_T",
            "weights",
            "mixed",
            "mixed_read",
            "rotated",
            "key_scores",
            "key_scores_read",
            "row_used",
            "picked",
            "dots_moved",
            "row_asked",
            "numbers",
            "gelu",
            "gate_exp_in", "gate_exp",
            "decay_x", "decay_l",
            "gate_mm",
            "running",
            "diag_in", "diag_exp", "diag_ready", "diag_mm",
            "qs_in", "qs_exp", "qs_ready",
            "ks_in", "ks_exp", "ks_ready", "off_mm",
            "att_ready", "gla_mm", "gla_read", "out_gate",
            "conv_done",
            "dve_chain", "act_chain", "pool_chain",
            "consts",
            "trig_in", "trig", "lam_in", "lam_exp",
            "params", "keys_in", "stored")}
        wide_in = [sem(f"wide_in{i}") for i in range(GSLOTS)]
        deep_in = [sem(f"deep_in{i}") for i in range(DSLOTS)]
        gain_in = [sem(f"gain_in{i}") for i in range(2)]
        row_in = [sem(f"row_in{i}") for i in range(ROWSLOTS)]

        def seen(count):
            return max(count, 0)

        class Chain:

            def __init__(self, eng, name):
                self.eng, self.name, self.n = eng, name, 0

            def __call__(self, ins):
                self.n += 1
                ins.then_inc(S[self.name], 1)
                self.eng.wait_ge(S[self.name], self.n)

        def ds(at, n):
            return bass.ds(at, n)

        def panels(ph):
            def of(kind, w, kt, src):
                return [(w, kt, src, c0, n, lay) for c0, n, lay in panels_of(kind)]
            if ph.kind == "sb":
                return of("sb", A["sb_w_qkv"][ph.j], KT, xT)
            if ph.kind == "moba":
                return of("moba", A["moba_w_qkv"][ph.j], KT, xT)
            if ph.kind == "mla":
                return (of("mla_in", A["mla_w_in"][ph.j], KT, xT)
                        + of("mla_uq", A["mla_w_uq"][ph.j], 3, ml_cT[:, 0:3])
                        + of("mla_ukv", A["mla_w_ukv"][ph.j], 2, ml_cT[:, 3:5]))
            if ph.kind == "mix2":
                return of("mix2", A["w_in_2"][ph.i], KT, xT)
            if ph.kind == "peer":
                return of("pq", A["peer_w_q_2"][ph.i], KT, xT)
            return []

        def out_weights(ph):
            return {"sb": lambda: A["sb_w_o"][ph.j], "moba": lambda: A["moba_w_o"][ph.j],
                    "mla": lambda: A["mla_w_o"][ph.j], "mix2": lambda: A["w_out_2"][ph.i]}[ph.kind]()

        mo_groups = [[mo_qk[:, t, c * P:(c + 1) * P] for c in (2 * g, 2 * g + 1) for t in range(TT)]
                     for g in range(KT)]
        ml_c_groups = [[ml_c[:, t, c * P:(c + 1) * P] for c in cs for t in range(TT)]
                       for cs in ((0,), (1,), (2,), (3, 4))]
        ml_groups = [[m[:, t, h] for m in (ml_q, ml_k) for t in range(TT)] for h in range(HEADS)]
        m2_qk_groups = [[m2_qk[:, t, c * P:(c + 1) * P] for c in (2 * g, 2 * g + 1)
                         for t in range(TT)] for g in range(4)]
        m2_out_groups = ([[m2_od[:, t, c * P:(c + 1) * P] for c in (2 * g, 2 * g + 1)
                           for t in range(TT)] for g in range(2)]
                         + [[m2_og[:, t, c * P:(c + 1) * P] for t in range(TT)] for c in range(2)])
        pk_groups = [[pk_keys[:, m]] for m in range(2)]

        def turned_to(ph, g):
            if ph.kind == "norm":
                t, half = g // 2, g % 2
                return P, xT[:, 4 * half:4 * half + 4, t * P:(t + 1) * P], 512
            if ph.kind == "moba":
                return P, mo_T[:, 2 * g:2 * g + 2].rearrange("p c t -> p (c t)"), 512
            if ph.kind == "mla":
                if g < 4:
                    n = 1 + (g == 3)
                    return P, ml_cT[:, g:g + n].rearrange("p c t -> p (c t)"), n * TOK
                return MLA_QK, ml_T[0:MLA_QK, g - 4], 512
            if ph.kind == "mix2":
                if g < 4:
                    return P, m2_qkT[:, 2 * g:2 * g + 2].rearrange("p c t -> p (c t)"), 512
                c, n = ((0, 2), (2, 2), (6, 1), (7, 1))[g - 4]
                return P, m2_mixT[:, c:c + n].rearrange("p c t -> p (c t)"), n * TOK
            return P, pk_keysT[:, g], P

        def move_turned(eng, ph, groups, op, name):
            for g in groups:
                n = ph.at.get("turned", 0) + g
                if n % 2 != (0 if name == "turned_act" else 1):
                    continue
                parts, dst, cols = turned_to(ph, g)
                eng.wait_ge(S["turned"], seen(n + 1))
                src = work[n % 4][0:parts, 0:cols]
                if len(dst.shape) == 3:
                    src = src.rearrange("p (a b) -> p a b", a=dst.shape[1])
                op(dst, src).then_inc(S[name], 1)

        wide_dmas, n = [], [0] * GSLOTS
        for ph in phases:
            for k in range(RAISES[ph.kind].get("wide", 0) // 2):
                g = ph.at.get("wide", 0) // 2 + k
                n[g % GSLOTS] += 2 if ph.kind == "ffn" else 1
                wide_dmas.append(n[g % GSLOTS])

        def wait_resid(eng, ph):
            eng.wait_ge(S["params"], 16 * N_PARAMS)
            eng.wait_ge(S["resid"], ph.at.get("resid", 0))
            eng.wait_ge(S["normed"], ph.at.get("normed", 0))
            eng.wait_ge(S["row_used"], ph.at.get("row_used", 0))

        N_PARAMS = 4 + DEPTH2 * 9 + 1

        block = ctx.enter_context(nc.Block())

        @block.sync
        def _(sp):
            def load_wide(ph, k, dst_src):
                g = ph.at.get("wide", 0) // 2
                slot = (g + (k if isinstance(k, int) else k[1])) % GSLOTS
                n = k if isinstance(k, int) else k[0]
                sp.wait_ge(S["wide"], seen(ph.at.get("wide", 0) + 2 * (n - GSLOTS + 1)))
                for dst, src in dst_src(slot):
                    sp.dma_start(dst, src).then_inc(wide_in[slot], 16)

            def load_deep(ph, k, w):
                d = ph.at.get("deep", 0)
                slot = (d + (k if isinstance(k, int) else k[1])) % DSLOTS
                n = k if isinstance(k, int) else k[0]
                sp.wait_ge(S["deep"], seen(d + n - DSLOTS + 1))
                src = w.rearrange("(s c p) n -> s p c n", p=P, c=DROWS // P)
                sp.dma_start(deep_ring[:, slot], src[n] if isinstance(n, int) else
                             src[ds(n, 1)].rearrange("s p c n -> (s p) c n")).then_inc(deep_in[slot], 16)

            for ph in phases:
                if ph.kind == "ffn":
                    up = A[f"ffn{ph.which}_w_gate_up"][ph.i].rearrange(
                        "(k p) (u n) -> p k u n", p=P, u=2)
                    down = A[f"ffn{ph.which}_w_down"][ph.i]

                    def gate_up(n):
                        def both(slot):
                            dst = wide_ring[:, slot].rearrange("p k (u n) -> p k u n", u=2)
                            return [(dst[:, :, u], up[:, :, u, ds(n * FFN_STEP, FFN_STEP)])
                                    for u in range(2)]
                        return both

                    def step(n, s):
                        load_wide(ph, (n, s), gate_up(n))
                        load_deep(ph, (n, s), down)

                    head = 4 if ph.at.get("wide", 0) == 0 else 3
                    for s in range(head):
                        step(s, s)
                    if head == 3:
                        with sp.Fori(0, 2) as r:
                            for s in range(3, 7):
                                step(r * 4 + s, s)
                    else:
                        for s in range(head, FFN_STEPS):
                            step(s, s)
                elif ph.kind in ("sb", "moba", "mla", "mix2", "peer"):
                    if ph.kind == "mix2" and ph.i > 0:
                        sp.wait_ge(S["row_used"], ph.at["row_used"])
                    for k, (w, kt, _, c0, n, _) in enumerate(panels(ph)):
                        def cols(slot, w=w, kt=kt, c0=c0, n=n):
                            return [(wide_ring[:, slot, 0:kt, 0:n],
                                     w.rearrange("(k p) n -> p k n", p=P)[:, :, c0:c0 + n])]
                        load_wide(ph, k, cols)
                    if ph.kind != "peer":
                        for k in range(4):
                            load_deep(ph, k, out_weights(ph))
            last = phases[-1]
            if last.kind == "norm_final":
                sp.wait_ge(S["normed"], last.at["normed"] + 2)
                src = xn
            else:
                sp.wait_ge(S["resid"], last.at.get("resid", 0) + RAISES[last.kind].get("resid", 0))
                src = resid
            sp.dma_start(out[0].rearrange("(t p) d -> p t d", p=P), src[:]).then_inc(S["stored"], 16)
            sp.wait_ge(S["stored"], 16)

        @block.tensor
        def _(pe):
            mm = nc.tensor.matmul

            def await_wide(ph, k, r=None):
                g = ph.at.get("wide", 0) // 2 + k
                need = 16 * wide_dmas[g]
                pe.wait_ge(wide_in[g % GSLOTS], need if r is None else r * 32 + need)

            def await_deep(ph, k, r=None):
                d = ph.at.get("deep", 0) + k
                need = 16 * (d // DSLOTS + 1)
                pe.wait_ge(deep_in[d % DSLOTS], need if r is None else r * 32 + need)

            def wide_products(ph):
                for k, (_, kt, src, c0, n, layout) in enumerate(panels(ph)):
                    if ph.kind == "mla" and k == 2:
                        pe.wait_ge(S["rotated"], ph.at["rotated"] + 1)
                        turn_groups(ph, 0, ml_c_groups)
                        pe.wait_ge(S["turned_act"], ph.at["turned_act"] + 2)
                        pe.wait_ge(S["turned_dve"], ph.at["turned_dve"] + 2)
                    slot = (ph.at["wide"] // 2 + k) % GSLOTS
                    await_wide(ph, k)
                    for j in range(2):
                        t = ph.at["wide"] + 2 * k + j
                        pe.wait_ge(S["wide_read"], seen(t - 3))
                        b, w = work[t % 4], wide_ring[:, slot]
                        if layout == "rows":
                            for c in range(kt):
                                ins = mm(b[:, 0:n], src[:, c, j * P:(j + 1) * P], w[:, c, 0:n],
                                         start=c == 0, stop=c == kt - 1)
                        elif layout == "T":
                            for i in range(2):
                                m = (2 * j + i) * P
                                for c in range(kt):
                                    ins = mm(b[:, i * TOK:(i + 1) * TOK], w[:, c, m:m + P], src[:, c, :],
                                             start=c == 0, stop=c == kt - 1)
                        else:
                            for c in range(kt):
                                ins = mm(b[0:n, 0:P], w[:, c, 0:n], src[:, c, j * P:(j + 1) * P],
                                         start=c == 0, stop=c == kt - 1)
                        ins.then_inc(S["wide"], 1)

            def deep_product(ph, k, last, lhs, r=None):
                await_deep(ph, k, r)
                w = deep_ring[:, (ph.at.get("deep", 0) + k) % DSLOTS]
                for c in range(2):
                    for t in range(TT):
                        for h in range(2):
                            ins = mm(acc[t][h][:, :], lhs(c)[:, t * P:(t + 1) * P],
                                     w[:, c, h * 512:(h + 1) * 512],
                                     start=k == 0 and c == 0 and r is None,
                                     stop=last and c == 1, skip_group_check=True)
                ins.then_inc(S["deep"], 1)

            def turn_groups(ph, first, groups):
                for g, tiles in enumerate(groups):
                    n = ph.at["turned"] + first + g
                    pe.wait_ge(S["turned_act" if n % 2 == 0 else "turned_dve"], seen((n - 4) // 2 + 1))
                    for i, src in enumerate(tiles):
                        ins = nc.tensor.transpose(work[n % 4][0:src.shape[1], i * P:(i + 1) * P],
                                                  src, ident[:])
                    ins.then_inc(S["turned"], 1)

            def norm(ph):
                for t in range(TT):
                    pe.wait_ge(S["normed"], ph.at.get("normed", 0) + t + 1)
                    for half in range(2):
                        g = ph.at.get("turned", 0) + 2 * t + half
                        pe.wait_ge(S["turned_act" if g % 2 == 0 else "turned_dve"], seen((g - 4) // 2 + 1))
                        for i in range(4):
                            c = 4 * half + i
                            ins = nc.tensor.transpose(work[g % 4][:, i * P:(i + 1) * P],
                                                      xn[:, t, c * P:(c + 1) * P], ident[:])
                        ins.then_inc(S["turned"], 1)
                pe.wait_ge(S["turned_act"], ph.at.get("turned_act", 0) + 2)
                pe.wait_ge(S["turned_dve"], ph.at.get("turned_dve", 0) + 2)

            def ffn(ph):
                def gate_up(s, r=None):
                    await_wide(ph, s, r)
                    w = wide_ring[:, (ph.at.get("wide", 0) // 2 + s) % GSLOTS]
                    for j in range(2):
                        t = ph.at.get("wide", 0) + 2 * s + j
                        if r is None:
                            pe.wait_ge(S["wide_read"], seen(t - 3))
                        else:
                            pe.wait_ge(S["wide_read"], r * 8 + (t - 3))
                        for u in range(2):
                            for c in range(KT):
                                m = u * FFN_STEP + j * P
                                ins = mm(work[t % 4][:, u * TOK:(u + 1) * TOK], w[:, c, m:m + P],
                                         xT[:, c, :], start=c == 0, stop=c == KT - 1)
                        ins.then_inc(S["wide"], 1)

                def down(s, r=None):
                    need = ph.at.get("wide", 0) + 2 * (s + 1)
                    pe.wait_ge(S["wide_read"], need if r is None else r * 8 + need)
                    t0 = ph.at.get("wide", 0) + 2 * s
                    await_deep(ph, s, r)
                    w = deep_ring[:, (ph.at.get("deep", 0) + s) % DSLOTS]
                    for c in range(2):
                        for t in range(TT):
                            for h in range(2):
                                ins = mm(acc[t][h][:, :], hidden[:, (t0 + c) % 4, t * P:(t + 1) * P],
                                         w[:, c, h * 512:(h + 1) * 512],
                                         start=s == 0 and c == 0 and r is None,
                                         stop=s == FFN_STEPS - 1 and c == 1, skip_group_check=True)
                    ins.then_inc(S["deep"], 1)

                for s in range(3):
                    gate_up(s)
                    if s:
                        down(s - 1)
                with pe.Fori(0, 2) as r:
                    for s in range(3, 7):
                        gate_up(s, r)
                        down(s - 1, r)
                down(FFN_STEPS - 1)

            def out_product(ph, k, src):
                deep_product(ph, k, k == 3, lambda c: src[:, 2 * k + c, :])

            def stick_breaking(ph):
                wide_products(ph)
                pe.wait_ge(S["wide_read"], ph.at["wide_read"] + 12)
                at = ph.at

                def scores(h):
                    pe.wait_ge(S["masked"], seen(at.get("masked", 0) + h - 1))
                    p0, c = HD * (h % 2), h // 2
                    q, k = sb_qT[p0:p0 + HD, c], sb_kT[p0:p0 + HD, c]
                    mm(work[h % 2][:, 0:TOK], k[:, 0:P], q, start=True, stop=True)
                    mm(work[h % 2][:, TOK:TRI], k[:, P:TOK], q[:, P:TOK], start=True,
                       stop=True).then_inc(S["scores"], 1)

                def tails(h):
                    pe.wait_ge(S["softplus"], at.get("softplus", 0) + h + 1)
                    pe.wait_ge(S["tail_read"], at.get("tail_read", 0) + h)
                    sp_ = core_c[:, h % 2]
                    mm(work[2][:, 0:P], later[:], sp_[:, 0:P], start=True, stop=True)
                    mm(work[2][:, P:TOK], later[:], sp_[:, P:TOK], start=True, stop=False,
                       skip_group_check=True)
                    mm(work[2][:, P:TOK], ones[:], sp_[:, TOK:TRI], start=False, stop=True,
                       skip_group_check=True)
                    mm(work[2][:, TOK:TRI], later[:], sp_[:, TOK:TRI], start=True, stop=True,
                       skip_group_check=True).then_inc(S["tail"], 1)

                for i in range(HEADS + 3):
                    if i < HEADS:
                        scores(i)
                    if 0 <= i - 1 < HEADS:
                        tails(i - 1)
                    if 0 <= i - 2 < HEADS:
                        mix_values(ph, i - 2, sb_v, core_e)
                    if i >= 6 and (i - 6) % 4 == 0:
                        pe.wait_ge(S["mixed_read"], seen(at.get("mixed_read", 0) + i - 2))
                        out_product(ph, (i - 6) // 4, oT)

            def mix_values(ph, h, v, w):
                pe.wait_ge(S["weights"], ph.at.get("weights", 0) + h + 1)
                pe.wait_ge(S["mixed_read"], ph.at.get("mixed_read", 0) + h)
                o, w, c = work[3][:, (h % 2) * TOK:(h % 2 + 1) * TOK], w[:, h % 2], (h // 2) * P
                mm(o[:, 0:P], v[:, 0, c:c + P], w[:, 0:P], start=True, stop=True, skip_group_check=True)
                mm(o[:, P:TOK], v[:, 0, c:c + P], w[:, P:TOK], start=True, stop=False,
                   skip_group_check=True)
                mm(o[:, P:TOK], v[:, 1, c:c + P], w[:, TOK:TRI], start=False, stop=True,
                   skip_group_check=True).then_inc(S["mixed"], 1)

            def soft_scores(ph, u, q, k):
                pe.wait_ge(S["masked"], seen(ph.at.get("masked", 0) + u - 1))
                mm(work[u % 2][:, 0:P], q[:, 0:P], k[:, 0:P], start=True, stop=True)
                mm(work[u % 2][:, P:TRI], q[:, P:TOK], k, start=True, stop=True).then_inc(S["scores"], 1)

            def turn_probs(ph, u, n):
                pe.wait_ge(S["probs"], ph.at.get("probs", 0) + u + 1)
                pe.wait_ge(S["weights"], ph.at.get("weights", 0) + n)
                for i in range(3):
                    ins = nc.tensor.transpose(work[2][:, i * P:(i + 1) * P],
                                              core_b[:, u % 2, i * P:(i + 1) * P], ident[:])
                ins.then_inc(S["probs_T"], 1)

            def softmax_heads(ph, qk, v, o):
                for i in range(HEADS + 3):
                    if i < HEADS:
                        soft_scores(ph, i, *qk(i))
                    if 0 <= i - 1 < HEADS:
                        turn_probs(ph, i - 1, i - 1)
                    if 0 <= i - 2 < HEADS:
                        mix_values(ph, i - 2, v, core_c)
                    if i >= 6 and (i - 6) % 4 == 0:
                        pe.wait_ge(S["mixed_read"], seen(ph.at.get("mixed_read", 0) + i - 2))
                        out_product(ph, (i - 6) // 4, o)

            def block_attention(ph):
                wide_products(ph)
                pe.wait_ge(S["rotated"], ph.at.get("rotated", 0) + 1)
                pe.wait_ge(S["wide_read"], ph.at["wide_read"] + 12)
                turn_groups(ph, 0, mo_groups)
                pe.wait_ge(S["turned_act"], ph.at["turned_act"] + 4)
                pe.wait_ge(S["turned_dve"], ph.at["turned_dve"] + 4)

                def qk(h):
                    p0, c = HD * (h % 2), h // 2
                    return mo_T[p0:p0 + HD, c], mo_T[p0:p0 + HD, KT + c]
                softmax_heads(ph, qk, mo_v, oT)

            def latent_attention(ph):
                wide_products(ph)
                pe.wait_ge(S["rotated"], ph.at["rotated"] + 3)
                pe.wait_ge(S["wide_read"], ph.at["wide_read"] + 18)
                turn_groups(ph, 4, ml_groups)
                pe.wait_ge(S["turned_act"], ph.at["turned_act"] + 10)
                pe.wait_ge(S["turned_dve"], ph.at["turned_dve"] + 10)

                def qk(h):
                    return ml_T[0:MLA_QK, h, 0:TOK], ml_T[0:MLA_QK, h, TOK:2 * TOK]
                softmax_heads(ph, qk, ml_v, ml_oT)

            def parallel_mixer(ph):
                at = ph.at
                i = ph.i
                wide_products(ph)
                pe.wait_ge(S["wide_read"], at["wide_read"] + 14)
                mm(work[0][:, 0:TOK], gate2[:, i], m2_lr[0:GLA_RANK], start=True,
                   stop=True).then_inc(S["gate_mm"], 1)
                for t in range(TT):
                    pe.wait_ge(S["diag_ready"], 2 * i + t + 1)
                    for ii in range(SUB):
                        ins = mm(work[1][:, (t * SUB + ii) * 4:(t * SUB + ii) * 4 + 4],
                                 m2_diag[:, t, ii].rearrange("p n j -> p (n j)"), head_of[:],
                                 start=True, stop=True, skip_group_check=True)
                    ins.then_inc(S["diag_mm"], 1)
                pe.wait_ge(S["qs_ready"], i + 1)
                for n in range(1, 2 * NSUB):
                    pe.wait_ge(S["ks_ready"], seen(15 * i + n))
                    slot = (n + 15 * i) % 4
                    q = m2_qsb[:, n].rearrange("p h i -> p (h i)")
                    at_n = (n % NSUB) * 64
                    ins = mm(work[2 + n // NSUB][:, at_n:at_n + 64], m2_ks[:, slot, 0:P], q,
                             start=True, stop=True, skip_group_check=True)
                    if n > NSUB:
                        ins = mm(bank[0][:, at_n:at_n + 64], m2_ks[:, slot, P:TOK], q,
                                 start=True, stop=True, skip_group_check=True)
                    ins.then_inc(S["off_mm"], 1)
                pe.wait_ge(S["att_ready"], i + 1)
                for t in range(TT):
                    for h in range(GLA_HEADS):
                        o = bank[1][:, t * 256 + h * 64:t * 256 + h * 64 + 64]
                        for kt in range(t + 1):
                            ins = mm(o, m2_AT[:, 0 if t == 0 else 1 + kt, h],
                                     m2_gv[:, kt, h * 64:h * 64 + 64], start=kt == 0, stop=kt == t,
                                     skip_group_check=True)
                ins.then_inc(S["gla_mm"], 1)
                pe.wait_ge(S["rotated"], at["rotated"] + 1)
                turn_groups(ph, 0, m2_qk_groups)
                pe.wait_ge(S["turned_act"], at["turned_act"] + 2)
                pe.wait_ge(S["turned_dve"], at["turned_dve"] + 2)
                for u in range(2 * DA_HEADS + 3):
                    if u < 2 * DA_HEADS:
                        p0, c = 64 * (u % 2), u // 2
                        soft_scores(ph, u, m2_qkT[p0:p0 + 64, c], m2_qkT[p0:p0 + 64, 4 + c])
                    if u >= 2 and u % 2 == 0 and u // 2 <= DA_HEADS:
                        turn_probs(ph, u - 1, u // 2 - 1)
                    if u >= 3 and u % 2 == 1:
                        h = (u - 3) // 2
                        pe.wait_ge(S["weights"], at.get("weights", 0) + h + 1)
                        pe.wait_ge(S["mixed_read"], at.get("mixed_read", 0) + h)
                        o, w = work[3][:, (h % 2) * 256:(h % 2) * 256 + 256], core_c[:, h % 2]
                        v = m2_v[:, :, h * DA_V:(h + 1) * DA_V]
                        mm(o[:, 0:P], w[:, 0:P], v[:, 0], start=True, stop=True, skip_group_check=True)
                        mm(o[:, P:256], w[:, P:TOK], v[:, 0], start=True, stop=False,
                           skip_group_check=True)
                        mm(o[:, P:256], w[:, TOK:TRI], v[:, 1], start=False, stop=True,
                           skip_group_check=True).then_inc(S["mixed"], 1)
                pe.wait_ge(S["rotated"], at["rotated"] + 2)
                turn_groups(ph, 4, m2_out_groups)
                pe.wait_ge(S["turned_act"], at["turned_act"] + 4)
                pe.wait_ge(S["turned_dve"], at["turned_dve"] + 4)
                pe.wait_ge(S["conv_done"], i + 1)
                for k in range(4):
                    out_product(ph, k, m2_mixT)

            def product_keys(ph):
                wide_products(ph)
                pe.wait_ge(S["keys_in"], 32 * (ph.i + 1))
                pe.wait_ge(S["wide_read"], ph.at["wide_read"] + 8)
                turn_groups(ph, 0, pk_groups)
                pe.wait_ge(S["turned_act"], ph.at["turned_act"] + 1)
                pe.wait_ge(S["turned_dve"], ph.at["turned_dve"] + 1)
                for n in range(8):
                    t, g = n // 4, n % 4
                    pe.wait_ge(S["key_scores_read"], seen(8 * ph.i + n - 3 if n > 3 else 0))
                    for i in range(4):
                        c = 4 * g + i
                        ins = mm(work[n % 4][:, i * P:(i + 1) * P], pk_qT[:, c, t * P:(t + 1) * P],
                                 pk_keysT[:, c % 2], start=True, stop=True, skip_group_check=True)
                    ins.then_inc(S["key_scores"], 1)

            pe.wait_ge(S["consts"], 1)
            for ph in phases:
                {"norm": norm, "norm_final": lambda ph: None, "ffn": ffn, "sb": stick_breaking,
                 "moba": block_attention, "mla": latent_attention, "mix2": parallel_mixer,
                 "peer": product_keys}[ph.kind](ph)

        @block.scalar
        def _(act):
            chain = Chain(act, "act_chain")
            A_ = nc.scalar.activation

            def move(dst, src):
                return A_(dst, src, ACT.Copy)

            def rows(ap):
                return ap.partition_broadcast(P)
            n = [0]

            def param(dst, src):
                act.dma_start(dst, src, allow_slow_non_contiguous=True).then_inc(S["params"], 16)
                n[0] += 16
            act.dma_start(resid[:], A["x"][0].rearrange("(t p) d -> p t d", p=P)).then_inc(S["params"], 16)
            param(posi[:], A["positions_2"].rearrange("a (t p) -> p (a t)", p=P))
            param(mla_gain[:, 0:Q_RANK], rows(A["mla_q_norm"][0]))
            param(mla_gain[:, Q_RANK:], rows(A["mla_kv_norm"][0]))
            for i in range(DEPTH2):
                param(diff_gain[:, i], rows(A["diff_norm_2"][i]))
                param(gla_gain[:, i], rows(A["gla_norm_2"][i]))
                for m, nm in enumerate(("lam_q1_2", "lam_k1_2", "lam_q2_2", "lam_k2_2")):
                    param(lam_rows[:, i, m], rows(A[nm][i]))
                param(gate2[:, i], A["gla_w_gate2_2"][i])
                for c in range(2):
                    param(conv_taps[:, i, c], A["conv_w_2"][i].rearrange("j (c p) -> c p j", p=P)[c])
            param(gate_bias[:], A["gla_b_gate_2"].rearrange("l p -> p l"))

            def norm(ph):
                wait_resid(act, ph)
                for t in range(TT):
                    act.wait_ge(S["normed"], ph.at.get("normed", 0))
                    A_(xn[:, t], resid[:, t], ACT.Square,
                       accum_out=small[:, t:t + 1]).then_inc(S["square_sum"], 1)
                if ph.kind == "norm":
                    move_turned(act, ph, range(4), move, "turned_act")

            def ffn(ph):
                def silu(n, b, r=None):
                    at = ph.at.get("wide", 0)
                    if r is None:
                        act.wait_ge(S["wide"], seen(at + n + 1))
                        act.wait_ge(S["wide_read"], seen(at + n - 1))
                    else:
                        act.wait_ge(S["wide"], r * 4 + (at + n + 1))
                        act.wait_ge(S["wide_read"], r * 4 + (at + n - 1))
                    A_(silu_buf[:, (at + n) % 2], work[(at + n) % 4][:, 0:TOK],
                       ACT.Silu).then_inc(S["silu"], 1)
                for n in range(6):
                    silu(n, 0)
                with act.Fori(0, 4) as r:
                    for n in range(6, 10):
                        silu(n, 0, r)

            def stick_breaking(ph):
                at = ph.at
                for i in range(HEADS + 1):
                    if i < HEADS:
                        act.wait_ge(S["masked"], at.get("masked", 0) + i + 1)
                        act.wait_ge(S["softplus"], seen(at.get("softplus", 0) + i - 1))
                        l = core_b[:, i % 2]
                        chain(A_(l, core_a[:, i % 2], ACT.Abs))
                        chain(A_(l, l, ACT.Exp, scale=-1.0))
                        A_(l, l, ACT.Ln, bias=1.0).then_inc(S["log1p"], 1)
                    if i >= 1:
                        h = i - 1
                        act.wait_ge(S["tail_read"], at.get("tail_read", 0) + h + 1)
                        act.wait_ge(S["mixed"], seen(at.get("mixed", 0) + h - 1))
                        A_(core_e[:, h % 2], core_d[:, h % 2], ACT.Exp).then_inc(S["weights"], 1)

            def soft_exp(ph, u):
                act.wait_ge(S["row_max"], ph.at.get("row_max", 0) + u + 1)
                e, s = core_b[:, u % 2], core_a[:, u % 2]
                act.wait_ge(S["probs"], seen(ph.at.get("probs", 0) + u - 1))
                A_(e[:, 0:P], s[:, 0:P], ACT.Exp, bias=small[:, 8 + 2 * (u % 2):9 + 2 * (u % 2)],
                   accum_out=small[:, 12 + 2 * (u % 2):13 + 2 * (u % 2)])
                A_(e[:, P:TRI], s[:, P:TRI], ACT.Exp, bias=small[:, 9 + 2 * (u % 2):10 + 2 * (u % 2)],
                   accum_out=small[:, 13 + 2 * (u % 2):14 + 2 * (u % 2)]).then_inc(S["exps"], 1)

            def move_probs(ph, h):
                act.wait_ge(S["probs_T"], ph.at.get("probs_T", 0) + h + 1)
                act.wait_ge(S["mixed"], seen(ph.at.get("mixed", 0) + h - 1))
                A_(core_c[:, h % 2], work[2][:, 0:TRI], ACT.Copy).then_inc(S["weights"], 1)

            def softmax_heads(ph):
                for i in range(HEADS + 1):
                    if i < HEADS:
                        act.wait_ge(S["probs_T"], seen(ph.at.get("probs_T", 0) + i - 1))
                        soft_exp(ph, i)
                    if i >= 1:
                        move_probs(ph, i - 1)

            def block_attention(ph):
                move_turned(act, ph, range(8), move, "turned_act")
                softmax_heads(ph)

            def latent_attention(ph):
                move_turned(act, ph, range(20), move, "turned_act")
                softmax_heads(ph)

            def parallel_mixer(ph):
                i = ph.i
                act.wait_ge(S["decay_x"], i + 1)
                l = m2_la[:, 1]
                chain(A_(l, m2_la[:, 0], ACT.Abs))
                chain(A_(l, l, ACT.Exp, scale=-1.0))
                A_(l, l, ACT.Ln, bias=1.0).then_inc(S["decay_l"], 1)
                for t in range(TT):
                    act.wait_ge(S["diag_in"], 2 * i + t + 1)
                    d = m2_diag[:, t].rearrange("p a b c -> p (a b c)")
                    A_(d, d, ACT.Exp).then_inc(S["diag_exp"], 1)
                act.wait_ge(S["qs_in"], i + 1)
                A_(m2_la[:, 2], m2_la[:, 2], ACT.Exp).then_inc(S["qs_exp"], 1)
                for n in range(1, 2 * NSUB):
                    m = 15 * i + n
                    act.wait_ge(S["ks_in"], seen(m))
                    w = P if n <= NSUB else TOK
                    k = m2_ks[:, m % 4, 0:w]
                    A_(k, k, ACT.Exp, scale=-1.0).then_inc(S["ks_exp"], 1)
                act.wait_ge(S["wide_read"], ph.at["wide_read"] + 14)
                A_(m2_tmp[:, 0].rearrange("p (t n) -> p t n", t=TT), m2_gv[:, :, 256:512],
                   ACT.Silu).then_inc(S["out_gate"], 1)
                move_turned(act, ph, range(4), move, "turned_act")
                for u in range(2 * DA_HEADS + 1):
                    if u < 2 * DA_HEADS:
                        act.wait_ge(S["probs_T"], seen(ph.at.get("probs_T", 0) + u // 2))
                        soft_exp(ph, u)
                    if u >= 2 and u % 2 == 0:
                        move_probs(ph, u // 2 - 1)
                move_turned(act, ph, range(4, 8), move, "turned_act")

            def product_keys(ph):
                act.wait_ge(S["normed"], ph.at["normed"])
                act.dma_start(pk_keys[:, 0], A["peer_keys1_2"][ph.i]).then_inc(S["keys_in"], 16)
                act.dma_start(pk_keys[:, 1], A["peer_keys2_2"][ph.i]).then_inc(S["keys_in"], 16)
                move_turned(act, ph, range(2), move, "turned_act")
                for n in range(8):
                    act.wait_ge(S["key_scores"], seen(8 * ph.i + n + 1))
                    t, g = n // 4, n % 4
                    A_(pk_S[:, t, 4 * g:4 * g + 4].rearrange("p c n -> p (c n)"), work[n % 4][:, :],
                       ACT.Copy).then_inc(S["key_scores_read"], 1)
                for t in range(TT):
                    act.wait_ge(S["gate_exp_in"], seen(2 * ph.i + t + 1))
                    g = pk_gate[:, t]
                    A_(g, g, ACT.Exp).then_inc(S["gate_exp"], 1)
                for t in range(TT):
                    act.wait_ge(S["dots_moved"], seen(16 * (2 * ph.i + t) + 8))
                    act.wait_ge(S["row_used"], ph.at.get("row_used", 0) + 256 * t)
                    A_(pk_coef, pk_dot, ACT.Gelu).then_inc(S["gelu"], 1)

            act.wait_ge(S["trig_in"], 1)
            A_(trig[:].rearrange("p a t f -> p (a t f)"),
               ang[:, 2:4].rearrange("p a t f -> p (a t f)"), ACT.Sin).then_inc(S["trig"], 1)
            act.wait_ge(S["lam_in"], 1)
            A_(small[:, 24:28], small[:, 20:24], ACT.Exp).then_inc(S["lam_exp"], 1)
            for ph in phases:
                {"norm": norm, "norm_final": norm, "ffn": ffn, "sb": stick_breaking,
                 "moba": block_attention, "mla": latent_attention, "mix2": parallel_mixer,
                 "peer": product_keys}[ph.kind](ph)

        @block.vector
        def _(dve):
            V = nc.vector
            chain = Chain(dve, "dve_chain")

            def move(dst, src):
                return V.tensor_copy(dst, src)

            def take_wide(ph):
                for k, (_, _, _, c0, n, layout) in enumerate(panels(ph)):
                    if ph.kind == "mla" and k == 2:
                        latent_norms(ph)
                    for j in range(2):
                        t = ph.at["wide"] + 2 * k + j
                        dve.wait_ge(S["wide"], t + 1)
                        b = work[t % 4]
                        if ph.kind == "sb":
                            if layout == "T":
                                dst = (sb_qT if k < 2 else sb_kT)[:, 4 * (k % 2) + 2 * j:
                                                                  4 * (k % 2) + 2 * j + 2]
                                dst = dst.rearrange("p c t -> p (c t)")
                            else:
                                dst = sb_v[:, j, (k - 4) * 512:(k - 3) * 512]
                        elif ph.kind == "moba":
                            dst = (mo_qk[:, j, k * 512:(k + 1) * 512] if k < 4 else
                                   mo_v[:, j, (k - 4) * 512:(k - 3) * 512])
                        elif ph.kind == "mla":
                            if k < 2:
                                dst = ml_c[:, j, c0:c0 + n]
                            elif k < 5:
                                dst = ml_q[:, j].rearrange("p h d -> p (h d)")[:, (k - 2) * 512:(k - 1) * 512]
                            else:
                                h0 = 4 * (k - 5)
                                s = b[:, :].rearrange("p (h x) -> p h x", h=4)
                                V.tensor_copy(ml_k[:, j, h0:h0 + 4, 0:64], s[:, :, 0:64])
                                V.tensor_copy(ml_v[:, j, h0 * 64:(h0 + 4) * 64].rearrange(
                                    "p (h x) -> p h x", h=4), s[:, :, 64:128]).then_inc(S["wide_read"], 1)
                                continue
                        elif ph.kind == "mix2":
                            if k < 2:
                                dst = m2_qk[:, j, k * 512:(k + 1) * 512]
                            elif k == 2:
                                dst = m2_v[:, j]
                            elif k == 3 or (k == 4 and j == 0):
                                c = 4 * (k - 3) + 2 * j
                                dst = m2_sc[:, c:c + 2].rearrange("p c t -> p (c t)")
                            elif k == 4:
                                dst = m2_gq.rearrange("p c t -> p (c t)")
                            elif k == 5:
                                dst = m2_gv[:, j]
                            else:
                                V.tensor_copy(m2_lr[0:GLA_RANK, j * P:(j + 1) * P],
                                              b[0:GLA_RANK, 0:P]).then_inc(S["wide_read"], 1)
                                continue
                        else:
                            c = 4 * k + 2 * j
                            dst = pk_qT[:, c:c + 2].rearrange("p c t -> p (c t)")
                        V.tensor_copy(dst, b[:, 0:n]).then_inc(S["wide_read"], 1)

            def norm(ph):
                at = ph.at
                gslot = at.get("gains", 0) % 2
                dve.wait_ge(S["square_sum"], at.get("square_sum", 0) + 2)
                V.tensor_scalar(small[:, 2:4], small[:, 0:2], 1.0 / D, EPS, ALU.mult,
                                ALU.add).then_inc(S["mean_square"], 1)
                dve.wait_ge(S["rstd"], at.get("rstd", 0) + 1)
                dve.wait_ge(gain_in[gslot], 16 * (at.get("gains", 0) // 2 + 1))
                to_resid = ph.kind == "norm_final" and not ph.last
                for t in range(TT):
                    V.scalar_tensor_tensor(out=(resid if to_resid else xn)[:, t], in0=resid[:, t],
                                           scalar=small[:, 4 + t:5 + t], in1=gains[:, gslot],
                                           op0=ALU.mult, op1=ALU.mult).then_inc(S["normed"], 1)
                if ph.kind == "norm":
                    move_turned(dve, ph, range(4), move, "turned_dve")

            def add_deep(ph, n, scale):
                dve.wait_ge(S["deep"], ph.at.get("deep", 0) + n)
                for t in range(TT):
                    for h in range(2):
                        r = resid[:, t, h * 512:(h + 1) * 512]
                        V.scalar_tensor_tensor(out=r, in0=acc[t][h][:, :], scalar=scale, in1=r,
                                               op0=ALU.mult, op1=ALU.add).then_inc(S["resid"], 1)

            def ffn(ph):
                def gated(n, r=None):
                    at, d = ph.at.get("wide", 0), ph.at.get("deep", 0)
                    k = ph.at.get("silu", 0) + n + 1
                    if r is None:
                        dve.wait_ge(S["silu"], seen(k))
                        dve.wait_ge(S["deep"], seen(d + n // 2 - 1))
                    else:
                        dve.wait_ge(S["silu"], r * 4 + k)
                        dve.wait_ge(S["deep"], r * 2 + (d + n // 2 - 1))
                    V.tensor_tensor(hidden[:, (at + n) % 4], work[(at + n) % 4][:, TOK:2 * TOK],
                                    silu_buf[:, (at + n) % 2], ALU.mult).then_inc(S["wide_read"], 1)
                for n in range(6):
                    gated(n)
                with dve.Fori(0, 4) as r:
                    for n in range(6, 10):
                        gated(n, r)
                add_deep(ph, FFN_STEPS, 0.5)

            def mixed_out(ph, h, o):
                dve.wait_ge(S["mixed"], ph.at.get("mixed", 0) + h + 1)
                p0 = HD * (h % 2)
                V.tensor_copy(o[p0:p0 + HD, h // 2], work[3][p0:p0 + HD, (h % 2) * TOK:(h % 2 + 1) * TOK]
                              ).then_inc(S["mixed_read"], 1)

            def stick_breaking(ph):
                at = ph.at
                take_wide(ph)
                for i in range(HEADS + 2):
                    if i < HEADS:
                        dve.wait_ge(S["scores"], at.get("scores", 0) + i + 1)
                        dve.wait_ge(S["tail_read"], seen(at.get("tail_read", 0) + i - 1))
                        V.scalar_tensor_tensor(out=core_a[:, i % 2], in0=work[i % 2][:, 0:TRI],
                                               scalar=HD ** -0.5, in1=mask_T[:], op0=ALU.mult,
                                               op1=ALU.add).then_inc(S["masked"], 1)
                    if 0 <= i - 1 < HEADS:
                        h = i - 1
                        dve.wait_ge(S["tail"], at.get("tail", 0) + h + 1)
                        dve.wait_ge(S["weights"], seen(at.get("weights", 0) + h - 1))
                        V.tensor_tensor(core_d[:, h % 2], core_a[:, h % 2], work[2][:, 0:TRI],
                                        ALU.subtract).then_inc(S["tail_read"], 1)
                    if 0 <= i - 2 < HEADS:
                        mixed_out(ph, i - 2, oT)
                    if i < HEADS:
                        dve.wait_ge(S["log1p"], at.get("log1p", 0) + i + 1)
                        dve.wait_ge(S["tail"], seen(at.get("tail", 0) + i - 1))
                        V.scalar_tensor_tensor(out=core_c[:, i % 2], in0=core_a[:, i % 2], scalar=0.0,
                                               in1=core_b[:, i % 2], op0=ALU.max,
                                               op1=ALU.add).then_inc(S["softplus"], 1)
                add_deep(ph, 4, 1.0)

            def soft_mask(ph, u, scale):
                dve.wait_ge(S["scores"], ph.at.get("scores", 0) + u + 1)
                dve.wait_ge(S["exps"], seen(ph.at.get("exps", 0) + u - 1))
                V.scalar_tensor_tensor(out=core_a[:, u % 2], in0=work[u % 2][:, 0:TRI], scalar=scale,
                                       in1=mask_rows[:], op0=ALU.mult, op1=ALU.add
                                       ).then_inc(S["masked"], 1)
                dve.wait_ge(S["masked"], ph.at.get("masked", 0) + u + 1)
                m = 8 + 2 * (u % 2)
                V.tensor_reduce(small[:, m:m + 1], core_a[:, u % 2, 0:P], AX, ALU.max, negate=True)
                V.tensor_reduce(small[:, m + 1:m + 2], core_a[:, u % 2, P:TRI], AX, ALU.max,
                                negate=True).then_inc(S["row_max"], 1)

            def soft_norm(ph, u):
                dve.wait_ge(S["exps"], ph.at.get("exps", 0) + u + 1)
                m = 2 * (u % 2)
                chain(V.reciprocal(small[:, 16 + m:18 + m], small[:, 12 + m:14 + m]))
                e = core_b[:, u % 2]
                V.tensor_scalar(e[:, 0:P], e[:, 0:P], small[:, 16 + m:17 + m], None, ALU.mult)
                V.tensor_scalar(e[:, P:TRI], e[:, P:TRI], small[:, 17 + m:18 + m], None,
                                ALU.mult).then_inc(S["probs"], 1)

            def softmax_heads(ph, scale, o):
                for i in range(HEADS + 2):
                    if i < HEADS:
                        soft_mask(ph, i, scale)
                    if 0 <= i - 1 < HEADS:
                        soft_norm(ph, i - 1)
                    if 0 <= i - 2 < HEADS:
                        mixed_out(ph, i - 2, o)
                add_deep(ph, 4, 1.0)

            def rotate(x, t, f, at, tmp):
                heads = x.shape[1]
                a, b = x[:, :, 0:f], x[:, :, f:2 * f]
                cos = trig[:, 0, t, at:at + f].unsqueeze(1).to_broadcast([P, heads, f])
                sin = trig[:, 1, t, at:at + f].unsqueeze(1).to_broadcast([P, heads, f])
                tm = [tmp[:, i * heads * f:(i + 1) * heads * f].rearrange("p (h f) -> p h f", f=f)
                      for i in range(4)]
                V.tensor_tensor(tm[0], a, cos, ALU.mult)
                V.tensor_tensor(tm[1], b, sin, ALU.mult)
                V.tensor_tensor(tm[2], a, sin, ALU.mult)
                chain(V.tensor_tensor(tm[3], b, cos, ALU.mult))
                V.tensor_tensor(a, tm[0], tm[1], ALU.subtract)
                return V.tensor_tensor(b, tm[2], tm[3], ALU.add)

            def block_attention(ph):
                take_wide(ph)
                dve.wait_ge(S["wide_read"], ph.at["wide_read"] + 12)
                for t in range(TT):
                    x = mo_qk[:, t].rearrange("p (h d) -> p h d", d=HD)[:, :, 0:16]
                    ins = rotate(x, t, 8, FREQ_AT[0], mo_tmp)
                    if t == 0:
                        chain(ins)
                ins.then_inc(S["rotated"], 1)
                move_turned(dve, ph, range(8), move, "turned_dve")
                softmax_heads(ph, HD ** -0.5, oT)

            def rms_scales(ph, k, n, width, name_at):
                V.tensor_scalar(small[:, 48:48 + n], small[:, 32:32 + n], 1.0 / width, EPS, ALU.mult,
                                ALU.add).then_inc(S["mean_square"], 1)

            def latent_norms(ph):
                dve.wait_ge(S["wide_read"], ph.at["wide_read"] + 4)
                spans = [(0, Q_RANK), (Q_RANK, Q_RANK + KV_RANK)]
                for t in range(TT):
                    for s, (a, b) in enumerate(spans):
                        chain(V.tensor_tensor_reduce(
                            out=ml_k[:, 0].rearrange("p h d -> p (h d)")[:, 0:b - a],
                            in0=ml_c[:, t, a:b], in1=ml_c[:, t, a:b], scale=1.0 / (b - a), scalar=0.0,
                            op0=ALU.mult, op1=ALU.add, accum_out=small[:, 32 + 2 * t + s:33 + 2 * t + s]))
                V.tensor_scalar(small[:, 48:52], small[:, 32:36], EPS, None,
                                ALU.add).then_inc(S["mean_square"], 1)
                dve.wait_ge(S["rstd"], ph.at["rstd"] + 1)
                for t in range(TT):
                    for s, (a, b) in enumerate(spans):
                        V.scalar_tensor_tensor(out=ml_c[:, t, a:b], in0=ml_c[:, t, a:b],
                                               scalar=small[:, 52 + 2 * t + s:53 + 2 * t + s],
                                               in1=mla_gain[:, a:b], op0=ALU.mult, op1=ALU.mult)
                    r = ml_c[:, t, Q_RANK + KV_RANK:].unsqueeze(1)
                    chain(rotate(r, t, 16, FREQ_AT[1], ml_k[:, 1, 0:4].rearrange("p h d -> p (h d)")))
                V.tensor_copy(small[:, 60:61], small[:, 52:53]).then_inc(S["rotated"], 1)
                move_turned(dve, ph, range(4), move, "turned_dve")

            def latent_attention(ph):
                take_wide(ph)
                dve.wait_ge(S["wide_read"], ph.at["wide_read"] + 18)
                for t in range(TT):
                    r = ml_c[:, t, Q_RANK + KV_RANK:].unsqueeze(1).to_broadcast([P, HEADS, ROPE])
                    ins = V.tensor_copy(ml_k[:, t, :, 64:MLA_QK], r)
                ins.then_inc(S["rotated"], 1)
                for t in range(TT):
                    ins = rotate(ml_q[:, t, :, 64:MLA_QK], t, 16, FREQ_AT[1], ml_T[:, 0:2].rearrange(
                        "p a b -> p (a b)"))
                    if t == 0:
                        chain(ins)
                ins.then_inc(S["rotated"], 1)
                move_turned(dve, ph, range(4, 20), move, "turned_dve")
                softmax_heads(ph, MLA_QK ** -0.5, ml_oT)

            def parallel_mixer(ph):
                i, at = ph.i, ph.at
                take_wide(ph)
                dve.wait_ge(S["wide_read"], at["wide_read"] + 14)
                for c in range(2):
                    z = m2_sc[:, 2 + c]
                    y = m2_mixT[:, 4 + c]
                    chain(V.tensor_tensor(z, z, m2_sc[:, 4 + c], ALU.mult))
                    w = conv_taps[:, i, c]
                    chain(V.tensor_scalar(y, z, w[:, 2:3], None, ALU.mult))
                    for j in (1, 0):
                        s = 2 - j
                        chain(V.scalar_tensor_tensor(out=y[:, s:], in0=z[:, 0:TOK - s],
                                                     scalar=w[:, j:j + 1], in1=y[:, s:],
                                                     op0=ALU.mult, op1=ALU.add))
                    ins = V.tensor_tensor(y, y, m2_sc[:, c], ALU.mult)
                ins.then_inc(S["conv_done"], 1)
                dve.wait_ge(S["gate_mm"], i + 1)
                V.tensor_scalar(m2_la[:, 0], work[0][:, 0:TOK], gate_bias[:, i:i + 1], None,
                                ALU.add).then_inc(S["decay_x"], 1)
                dve.wait_ge(S["decay_l"], i + 1)
                chain(V.scalar_tensor_tensor(out=m2_la[:, 0], in0=m2_la[:, 0], scalar=0.0,
                                             in1=m2_la[:, 1], op0=ALU.min, op1=ALU.subtract))
                chain(V.tensor_scalar(m2_la[:, 0], m2_la[:, 0], 1.0 / GLA_TEMP, None, ALU.mult))
                chain(V.tensor_tensor_scan(m2_b, m2_la[:, 0], zeros_tok[:], 0.0, ALU.add, ALU.add))
                b = m2_b
                q, k = m2_gq[:, 0], m2_gq[:, 1]
                chain(V.tensor_scalar(q, q, GLA_DK ** -0.5, None, ALU.mult))
                full = [P, SUB, NSUB, SUB]

                def by_i(v, t):
                    return v[:, t * P:(t + 1) * P].rearrange("p (n i) -> p i n", i=SUB).unsqueeze(
                        3).to_broadcast(full)

                def by_j(v, t):
                    return v[:, t * P:(t + 1) * P].rearrange("p (n j) -> p n j", j=SUB).unsqueeze(
                        1).to_broadcast(full)
                for t in range(TT):
                    d = m2_diag[:, t]
                    chain(V.tensor_tensor(d, by_i(b, t), by_j(b, t), ALU.subtract))
                    V.tensor_scalar(d, d, 0.0, None, ALU.min).then_inc(S["diag_in"], 1)
                e = m2_la[:, 2]
                chain(V.tensor_copy(e[:, 0:SUB], b[:, 0:SUB]))
                V.tensor_tensor(e[:, SUB:].rearrange("p (n i) -> p n i", i=SUB),
                                b[:, SUB:].rearrange("p (n i) -> p n i", i=SUB),
                                b[:, SUB - 1:TOK - SUB:SUB].unsqueeze(2).to_broadcast(
                                    [P, 2 * NSUB - 1, SUB]), ALU.subtract).then_inc(S["qs_in"], 1)
                for t in range(TT):
                    dve.wait_ge(S["diag_exp"], 2 * i + t + 1)
                    d = m2_diag[:, t]
                    chain(V.tensor_tensor(d, d, by_i(q, t), ALU.mult))
                    V.tensor_tensor(d, d, by_j(k, t), ALU.mult).then_inc(S["diag_ready"], 1)
                dve.wait_ge(S["qs_exp"], i + 1)
                chain(V.tensor_tensor(e, e, q, ALU.mult))
                for h in range(GLA_HEADS):
                    ins = V.tensor_scalar(m2_qsb[:, :, h, :], e.rearrange("p (n i) -> p n i", i=SUB),
                                          head_of[:, h:h + 1], None, ALU.mult)
                ins.then_inc(S["qs_ready"], 1)
                for n in range(1, 2 * NSUB + 2):
                    m = 15 * i + n
                    w = P if n <= NSUB else TOK
                    if n < 2 * NSUB:
                        dve.wait_ge(S["off_mm"], seen(m - 4))
                        V.tensor_scalar(m2_ks[:, m % 4, 0:w], b[:, 0:w], b[:, SUB * n - 1:SUB * n], 0.0,
                                        ALU.subtract, ALU.max).then_inc(S["ks_in"], 1)
                    if n >= 3:
                        m, w = m - 2, P if n - 2 <= NSUB else TOK
                        dve.wait_ge(S["ks_exp"], seen(m))
                        V.tensor_tensor(m2_ks[:, m % 4, 0:w], m2_ks[:, m % 4, 0:w], k[:, 0:w],
                                        ALU.mult).then_inc(S["ks_ready"], 1)
                dve.wait_ge(S["diag_mm"], seen(2 * (i + 1)))
                dve.wait_ge(S["off_mm"], seen(15 * (i + 1)))
                early = earlier_sub[:].unsqueeze(1).unsqueeze(3).to_broadcast([P, GLA_HEADS, NSUB, SUB])
                for blk, src in ((0, work[2]), (2, bank[0])):
                    dst = m2_AT[:, blk].rearrange("p h (n i) -> p h n i", i=SUB)
                    a = src[:, :].rearrange("p (n h i) -> p h n i", h=GLA_HEADS, i=SUB)
                    V.memset(dst[:, :, 0:1], 0.0)
                    V.tensor_tensor(dst[:, :, 1:], a[:, :, 1:], early[:, :, 1:], ALU.mult)
                chain(V.tensor_copy(m2_AT[:, 1].rearrange("p h (n i) -> p h n i", i=SUB),
                                    work[3][:, :].rearrange("p (n h i) -> p h n i", h=GLA_HEADS, i=SUB)))
                for t in range(TT):
                    g = work[1][:, t * 64:(t + 1) * 64].rearrange("p (i h) -> p h i", h=GLA_HEADS)
                    for h in range(GLA_HEADS):
                        gh = g[:, h].unsqueeze(1).to_broadcast([P, NSUB, SUB])
                        tmp = m2_tmp[:, 1, 0:P].rearrange("p (n i) -> p n i", i=SUB)
                        chain(V.tensor_tensor(tmp, gh, same_sub[:], ALU.mult))
                        a = m2_AT[:, 2 * t, h].rearrange("p (n i) -> p n i", i=SUB)
                        ins = V.tensor_tensor(a, a, tmp, ALU.add)
                        if (t, h) != (1, GLA_HEADS - 1):
                            chain(ins)
                ins.then_inc(S["att_ready"], 1)
                dve.wait_ge(S["gla_mm"], i + 1)
                og = m2_og.rearrange("p t n -> p (t n)")
                o4 = og.rearrange("p (g e) -> p g e", e=GLA_DV)
                t1 = m2_tmp[:, 1]
                chain(V.tensor_copy(og, bank[1][:, :]))
                chain(V.tensor_tensor(t1, og, og, ALU.mult))
                chain(V.tensor_reduce(small[:, 32:40], t1.rearrange("p (g e) -> p g e", e=GLA_DV), AX,
                                      ALU.add))
                V.tensor_scalar(small[:, 40:48], small[:, 32:40], 1.0 / GLA_DV, EPS, ALU.mult,
                                ALU.add).then_inc(S["mean_square"], 1)
                dve.wait_ge(S["rstd"], at["rstd"] + 1)
                chain(V.tensor_tensor(o4, o4, small[:, 48:56].unsqueeze(2).to_broadcast([P, 8, GLA_DV]),
                                      ALU.mult))
                chain(V.tensor_tensor(o4, o4, gla_gain[:, i].unsqueeze(1).to_broadcast([P, 8, GLA_DV]),
                                      ALU.mult))
                dve.wait_ge(S["out_gate"], i + 1)
                chain(V.tensor_tensor(og, og, m2_tmp[:, 0], ALU.mult))
                for t in range(TT):
                    x = m2_qk[:, t].rearrange("p (h d) -> p h d", d=64)[:, :, 0:16]
                    ins = rotate(x, t, 8, FREQ_AT[2], m2_tmp.rearrange("p a b -> p (a b)"))
                    if t == 0:
                        chain(ins)
                ins.then_inc(S["rotated"], 1)
                move_turned(dve, ph, range(4), move, "turned_dve")
                for u in range(2 * DA_HEADS + 3):
                    if u < 2 * DA_HEADS:
                        soft_mask(ph, u, 64 ** -0.5)
                    if 1 <= u <= 2 * DA_HEADS:
                        n = u - 1
                        if n % 2 == 0:
                            soft_norm(ph, n)
                        else:
                            dve.wait_ge(S["exps"], at.get("exps", 0) + n + 1)
                            chain(V.reciprocal(small[:, 18:20], small[:, 14:16]))
                            chain(V.tensor_scalar(small[:, 18:20], small[:, 18:20],
                                                  minus_lam[:, i:i + 1], None, ALU.mult))
                            e1, p0 = core_b[:, 1], core_b[:, 0]
                            V.scalar_tensor_tensor(out=e1[:, 0:P], in0=e1[:, 0:P], scalar=small[:, 18:19],
                                                   in1=p0[:, 0:P], op0=ALU.mult, op1=ALU.add)
                            V.scalar_tensor_tensor(out=e1[:, P:], in0=e1[:, P:], scalar=small[:, 19:20],
                                                   in1=p0[:, P:], op0=ALU.mult,
                                                   op1=ALU.add).then_inc(S["probs"], 1)
                    if u >= 4 and u % 2 == 0:
                        h = u // 2 - 2
                        dve.wait_ge(S["mixed"], at.get("mixed", 0) + h + 1)
                        V.tensor_copy(m2_od[:, :, h * DA_V:(h + 1) * DA_V],
                                      work[3][:, (h % 2) * 256:(h % 2) * 256 + 256].rearrange(
                                          "p (t e) -> p t e", t=TT)).then_inc(S["mixed_read"], 1)
                dve.wait_ge(S["mixed"], at.get("mixed", 0) + DA_HEADS)
                od = m2_od.rearrange("p t n -> p (t n)")
                o8 = od.rearrange("p (g e) -> p g e", e=DA_V)
                sq = m2_tmp.rearrange("p a b -> p (a b)")
                dve.wait_ge(S["mixed_read"], at.get("mixed_read", 0) + DA_HEADS)
                chain(V.tensor_tensor(sq, od, od, ALU.mult))
                chain(V.tensor_reduce(small[:, 32:40], sq.rearrange("p (g e) -> p g e", e=DA_V), AX,
                                      ALU.add))
                V.tensor_scalar(small[:, 40:48], small[:, 32:40], 1.0 / DA_V, EPS, ALU.mult,
                                ALU.add).then_inc(S["mean_square"], 1)
                dve.wait_ge(S["rstd"], at["rstd"] + 2)
                keep = 1.0 - (0.8 - 0.6 * math.exp(-0.3 * i))
                chain(V.tensor_scalar(small[:, 48:56], small[:, 48:56], keep, None, ALU.mult))
                chain(V.tensor_tensor(o8, o8, small[:, 48:56].unsqueeze(2).to_broadcast([P, 8, DA_V]),
                                      ALU.mult))
                V.tensor_tensor(o8, o8, diff_gain[:, i].unsqueeze(1).to_broadcast([P, 8, DA_V]),
                                ALU.mult).then_inc(S["rotated"], 1)
                move_turned(dve, ph, range(4, 8), move, "turned_dve")
                add_deep(ph, 4, 1.0)

            def top16(vals, idx, src):
                chain(V.max(vals[:, 0:8], src))
                V.max_index(idx[:, 0:8], vals[:, 0:8], src)
                chain(V.match_replace(src, vals[:, 0:8], src, -3e38))
                chain(V.max(vals[:, 8:16], src))
                chain(V.max_index(idx[:, 8:16], vals[:, 8:16], src))

            def pick(ph, t):
                dve.wait_ge(S["key_scores_read"], seen(8 * ph.i + 4 * (t + 1)))
                for c in range(16):
                    top16(pk_v[:, c], pk_i[:, c], pk_S[:, t, c])
                for h in range(PK_HEADS):
                    v1, v2 = pk_v[:, 2 * h], pk_v[:, 2 * h + 1]
                    chain(V.tensor_tensor(pk_cand.rearrange("p (a b) -> p a b", a=TOPK),
                                          v1.unsqueeze(2).to_broadcast([P, TOPK, TOPK]),
                                          v2.unsqueeze(1).to_broadcast([P, TOPK, TOPK]), ALU.add))
                    top16(pk_sc[:, h], pk_ci[:, h], pk_cand)
                g = pk_gate[:, t].rearrange("p (h s) -> p h s", s=TOPK)
                V.tensor_tensor(g, pk_sc, pk_sc[:, :, 0:1].to_broadcast([P, PK_HEADS, TOPK]),
                                ALU.subtract).then_inc(S["gate_exp_in"], 1)
                ci = pk_ci.rearrange("p h s -> p (h s)")
                V.tensor_scalar(pk_abu[:, 0], ci, 4, None, ALU.logical_shift_right)
                V.tensor_scalar(pk_abu[:, 1], ci, 15, None, ALU.bitwise_and)
                chain(V.tensor_copy(pk_if.rearrange("p a b -> p (a b)"),
                                    pk_i.rearrange("p a b -> p (a b)")))
                chain(V.tensor_copy(pk_ab.rearrange("p a b -> p (a b)"),
                                    pk_abu.rearrange("p a b -> p (a b)")))
                shape = [P, PICKS, TOPK]
                for m in range(2):
                    chain(V.tensor_tensor(pk_hot, pk_ab[:, m].unsqueeze(2).to_broadcast(shape),
                                          iota16[:].unsqueeze(1).to_broadcast(shape), ALU.is_equal))
                    hot = pk_hot.rearrange("p (h s) j -> p h s j", h=PK_HEADS)
                    which = pk_if.rearrange("p (h m) j -> p h m j", m=2)[:, :, m].unsqueeze(
                        2).to_broadcast([P, PK_HEADS, TOPK, TOPK])
                    chain(V.tensor_tensor(hot, hot, which, ALU.mult))
                    chain(V.tensor_reduce(pk_e[:, m], pk_hot, AX, ALU.add))
                chain(V.tensor_scalar(pk_e[:, 0], pk_e[:, 0], float(NKEYS), float(ph.i * EXPERTS),
                                      ALU.mult, ALU.add))
                V.tensor_tensor(pk_idx[:, t], pk_e[:, 0], pk_e[:, 1], ALU.add).then_inc(S["picked"], 1)
                dve.wait_ge(S["gate_exp"], seen(2 * ph.i + t + 1))
                chain(V.tensor_reduce(pk_den, g, AX, ALU.add))
                chain(V.reciprocal(pk_den, pk_den))
                chain(V.tensor_tensor(g, g, pk_den.unsqueeze(2).to_broadcast([P, PK_HEADS, TOPK]),
                                      ALU.mult))

            def product_keys(ph):
                take_wide(ph)
                move_turned(dve, ph, range(2), move, "turned_dve")
                for t in range(TT):
                    pick(ph, t)
                used = ph.at.get("row_used", 0)
                for t in range(TT):
                    with dve.Fori(0, PICKS // BURST) as r:
                        for n in range(BURST):
                            base = used + 256 * t
                            dve.wait_ge(row_in[n], r * 16 + (16 * (base // BURST) + 16))
                            V.tensor_tensor_reduce(out=pk_scratch, in0=row_ring[:, n], in1=xn[:, t],
                                                   scale=1.0, scalar=0.0, op0=ALU.mult, op1=ALU.add,
                                                   accum_out=pk_dots[:, 0, n:n + 1]
                                                   ).then_inc(S["row_used"], 1)
                            dve.wait_ge(S["row_used"], r * BURST + (base + n + 1))
                        V.tensor_copy(pk_dot[:, ds(r * BURST, BURST)], pk_dots[:, 0]
                                      ).then_inc(S["dots_moved"], 1)
                        dve.wait_ge(S["dots_moved"], r + (16 * (2 * ph.i + t) + 1))
                    dve.wait_ge(S["gelu"], seen(2 * ph.i + t + 1))
                    chain(V.tensor_tensor(pk_coef, pk_coef, pk_gate[:, t], ALU.mult))
                    with dve.Fori(0, PICKS // BURST) as r:
                        V.tensor_copy(pk_dots[:, 1], pk_coef[:, ds(r * BURST, BURST)]
                                      ).then_inc(S["dots_moved"], 1)
                        dve.wait_ge(S["dots_moved"], r + (16 * (2 * ph.i + t) + 9))
                        for n in range(BURST):
                            base = used + 256 * t + PICKS
                            dve.wait_ge(row_in[n], r * 16 + (16 * (base // BURST) + 16))
                            V.scalar_tensor_tensor(out=resid[:, t], in0=row_ring[:, n],
                                                   scalar=pk_dots[:, 1, n:n + 1], in1=resid[:, t],
                                                   op0=ALU.mult, op1=ALU.add
                                                   ).then_inc(S["row_used"], 1)
                            dve.wait_ge(S["row_used"], r * BURST + (base + n + 1))
            mo_tmp = cut(0, 2048)

            for i, r in enumerate(FREQS):
                for f in range(r // 2):
                    inv = float(np.float32(THETA) ** np.float32(-np.float32(2 * f) / np.float32(r)))
                    V.memset(inv_freq[:, FREQ_AT[i] + f:FREQ_AT[i] + f + 1], inv)
            dve.wait_ge(S["params"], 16 * N_PARAMS)
            chain(V.tensor_copy(posf[:, 1], posi[:]))
            dve.wait_ge(S["consts"], 1)
            for t in range(TT):
                for a, b, src in ((0, FREQ_AT[2], 0), (FREQ_AT[2], NFREQ, 1)):
                    ins = V.tensor_scalar(ang[:, 0, t, a:b], inv_freq[:, a:b], posf[:, src, t:t + 1],
                                          None, ALU.mult)
            chain(ins)
            big = 1.5 * 2.0 ** 23
            a0, a1, cs, sn = (ang[:, k] for k in range(4))
            chain(V.tensor_scalar(a1, a0, float(1 / (2 * math.pi)), big, ALU.mult, ALU.add))
            chain(V.tensor_scalar(a1, a1, big, None, ALU.subtract))
            two_pi = 2 * math.pi
            c1 = 6.28125
            c2 = float(np.float32(math.floor((two_pi - c1) * 2 ** 20) / 2 ** 20))
            c3 = two_pi - c1 - c2
            chain(V.scalar_tensor_tensor(out=sn, in0=a1, scalar=-c1, in1=a0, op0=ALU.mult, op1=ALU.add))
            chain(V.scalar_tensor_tensor(out=sn, in0=a1, scalar=-c2, in1=sn, op0=ALU.mult, op1=ALU.add))
            chain(V.scalar_tensor_tensor(out=sn, in0=a1, scalar=-c3, in1=sn, op0=ALU.mult, op1=ALU.add))
            lim = 3.1415925
            chain(V.tensor_scalar(cs, sn, math.pi / 2, None, ALU.add))
            chain(V.tensor_scalar(a1, cs, lim, -two_pi, ALU.is_gt, ALU.mult))
            chain(V.tensor_tensor(cs, cs, a1, ALU.add))
            chain(V.tensor_scalar(cs, cs, lim, -lim, ALU.min, ALU.max))
            V.tensor_scalar(sn, sn, lim, -lim, ALU.min, ALU.max).then_inc(S["trig_in"], 1)
            for i in range(DEPTH2):
                for m in range(2):
                    ins = V.tensor_tensor_reduce(out=ang[:, 0].rearrange("p t f -> p (t f)"),
                                                 in0=lam_rows[:, i, 2 * m], in1=lam_rows[:, i, 2 * m + 1],
                                                 scale=1.0, scalar=0.0, op0=ALU.mult, op1=ALU.add,
                                                 accum_out=small[:, 20 + 2 * i + m:21 + 2 * i + m])
                    if (i, m) != (1, 1):
                        chain(ins)
            ins.then_inc(S["lam_in"], 1)
            dve.wait_ge(S["lam_exp"], 1)
            for i in range(DEPTH2):
                chain(V.tensor_tensor(minus_lam[:, i:i + 1], small[:, 25 + 2 * i:26 + 2 * i],
                                      small[:, 24 + 2 * i:25 + 2 * i], ALU.subtract))
                chain(V.tensor_scalar(minus_lam[:, i:i + 1], minus_lam[:, i:i + 1],
                                      -(0.8 - 0.6 * math.exp(-0.3 * i)), None, ALU.add))
            dve.wait_ge(S["trig"], 1)
            for ph in phases:
                {"norm": norm, "norm_final": norm, "ffn": ffn, "sb": stick_breaking,
                 "moba": block_attention, "mla": latent_attention, "mix2": parallel_mixer,
                 "peer": product_keys}[ph.kind](ph)

        @block.gpsimd
        def _(pool):
            G = nc.gpsimd
            chain = Chain(pool, "pool_chain")

            def load_gain(ph):
                name, i = ph.gain
                g = ph.at.get("gains", 0)
                src = A[name] if i is None else A[name][i]
                pool.dma_start(gains[:, g % 2], src.partition_broadcast(P)).then_inc(gain_in[g % 2], 16)
            norms = [ph for ph in phases if ph.kind in ("norm", "norm_final")]
            for ph in norms[:2]:
                load_gain(ph)

            def select(m, pattern, op, fill, base, cm):
                chain(G.affine_select(out=m, in_=m, pattern=pattern, compare_op=op, fill=fill,
                                      base=base, channel_multiplier=cm))
            G.memset(ident[:], 0.0)
            G.memset(later[:], 1.0)
            G.memset(mask_T[:], 0.0)
            G.memset(mask_rows[:], 0.0)
            G.memset(head_of[:], 1.0)
            G.memset(earlier_sub[:], 1.0)
            G.memset(same_sub[:], 1.0)
            G.memset(minus_half[:], -0.5)
            G.memset(zeros_tok[:], 0.0)
            G.iota(iota16[:], pattern=[[1, TOPK]], base=0, channel_multiplier=0,
                   allow_small_or_imprecise_dtypes=True)
            G.iota(posf[:, 0], pattern=[[P, TT]], base=0, channel_multiplier=1,
                   allow_small_or_imprecise_dtypes=True)
            chain(G.memset(ones[:], 1.0))
            select(ident[:], [[-1, P]], ALU.not_equal, 1.0, 0, 1)
            select(later[:], [[-1, P]], ALU.is_ge, 0.0, 0, 1)
            select(mask_T[:, 0:TOK], [[1, TOK]], ALU.is_gt, NEG, 0, -1)
            select(mask_T[:, TOK:], [[1, P]], ALU.is_gt, NEG, 0, -1)
            select(mask_rows[:, 0:P], [[-1, P]], ALU.is_ge, NEG, 0, 1)
            select(mask_rows[:, P:], [[-1, TOK]], ALU.is_ge, NEG, P, 1)
            select(head_of[:], [[-GLA_DK, GLA_HEADS]], ALU.is_ge, 0.0, 0, 1)
            select(head_of[:], [[GLA_DK, GLA_HEADS]], ALU.is_ge, 0.0, GLA_DK - 1, -1)
            select(earlier_sub[:], [[SUB, NSUB]], ALU.is_gt, 0.0, 0, -1)
            select(same_sub[:], [[-SUB, NSUB], [0, SUB]], ALU.is_ge, 0.0, 0, 1)
            G.affine_select(out=same_sub[:], in_=same_sub[:], pattern=[[SUB, NSUB], [1, SUB]],
                            compare_op=ALU.is_ge, fill=0.0, base=0,
                            channel_multiplier=-1).then_inc(S["consts"], 1)

            def power(ph, k, dst, src):
                pool.wait_ge(S["mean_square"], ph.at.get("mean_square", 0) + k + 1)
                G.tensor_tensor(dst, src, minus_half[:, 0:src.shape[1]], ALU.pow).then_inc(S["rstd"], 1)

            def gather(ph):
                used = ph.at.get("row_used", 0)
                tables = [A["peer_u_2"].rearrange("l e d -> (l e) d"),
                          A["peer_v_2"].rearrange("l e d -> (l e) d")]
                pool.wait_ge(S["wide"], ph.at["wide"] + 8)
                for t in range(TT):
                    pool.wait_ge(S["picked"], seen(2 * ph.i + t + 1))
                    for m in range(2):
                        base = used + 256 * t + PICKS * m

                        def burst(r, parity, first):
                            c = r * (2 * BURST) + parity * BURST
                            G.tensor_copy(pk_burst[:, parity], pk_idx[:, t, ds(c, BURST)]
                                          ).then_inc(S["numbers"], 1)
                            k = (base // BURST) + parity + 1
                            pool.wait_ge(S["numbers"], r * 2 + k)
                            for n in range(BURST):
                                if not first:
                                    pool.wait_ge(S["row_used"],
                                                 r * 2 * BURST + (base + parity * BURST + n - BURST + 1))
                                    pool.sem_inc(S["row_asked"])
                                G.indirect_dma_start(
                                    row_ring[:, n], None, tables[m],
                                    bass.IndirectOffsetOnAxis(ap=pk_burst[:, parity, n:n + 1], axis=0)
                                ).then_inc(row_in[n], 16)
                        if base == 0:
                            burst(0, 0, True)
                            burst(0, 1, False)
                            with pool.Fori(1, PICKS // BURST // 2) as r:
                                for parity in range(2):
                                    burst(r, parity, False)
                        else:
                            with pool.Fori(0, PICKS // BURST // 2) as r:
                                for parity in range(2):
                                    burst(r, parity, False)
            for ph in phases:
                if ph.kind in ("norm", "norm_final"):
                    power(ph, 0, small[:, 4:6], small[:, 2:4])
                    k = norms.index(ph)
                    if k >= 1 and k + 1 < len(norms):
                        load_gain(norms[k + 1])
                elif ph.kind == "mla":
                    power(ph, 0, small[:, 52:56], small[:, 48:52])
                elif ph.kind == "mix2":
                    power(ph, 0, small[:, 48:56], small[:, 40:48])
                    power(ph, 1, small[:, 48:56], small[:, 40:48])
                elif ph.kind == "peer":
                    gather(ph)


_INS = ["x", "norm_ffn1", "ffn1_w_gate_up", "ffn1_w_down", "norm_mix", "norm_ffn2", "ffn2_w_gate_up",
        "ffn2_w_down", "sb_w_qkv", "sb_w_o", "moba_w_qkv", "moba_w_o", "mla_w_in", "mla_q_norm",
        "mla_w_uq", "mla_kv_norm", "mla_w_ukv", "mla_w_o", "final_norm", "positions_2", "norm_mix_2",
        "w_in_2", "lam_q1_2", "lam_k1_2", "lam_q2_2", "lam_k2_2", "diff_norm_2", "conv_w_2",
        "gla_w_gate2_2", "gla_b_gate_2", "gla_norm_2", "w_out_2", "norm_ffn_2", "peer_w_q_2",
        "peer_keys1_2", "peer_keys2_2", "peer_u_2", "peer_v_2", "norm_final_2"]
STOP = None


def kernel(**inputs):
    import concourse.bacc as _bacc
    from concourse import mybir as _mybir
    from concourse.bass_utils import run_bass_kernel_spmd as _run

    nc = _bacc.Bacc("TRN2", target_bir_lowering=False, num_devices=1)
    arrays, args = {}, {}
    for name in _INS:
        a = np.ascontiguousarray(inputs[name])
        arrays[f"in_{name}"] = a
        args[name] = nc.dram_tensor(f"in_{name}", a.shape, _mybir.dt.from_np(a.dtype),
                                    kind="ExternalInput").ap()
    out = nc.dram_tensor("out_0", (1, TOK, D), F32, kind="ExternalOutput").ap()
    build(nc, args, out, STOP)
    r = _run(nc, [arrays], core_ids=[0])
    return r.results[0]["out_0"]
```

```python
import math
from contextlib import ExitStack

import numpy as np

import concourse.bass as bass
from concourse import mybir

F32 = mybir.dt.float32
U32 = mybir.dt.uint32
I32 = mybir.dt.int32
F32R = mybir.dt.float32r
ALU = mybir.AluOpType
ACT = mybir.ActivationFunctionType
AX = mybir.AxisListType.X

P = 128
D = 1024
TOK = 256
TT = TOK // P
KT = D // P
HEADS = 16
HD = D // HEADS
DEPTH, DEPTH2 = 4, 2
D_FF = ((8 * D // 3 + 127) // 128) * 128
FFN_STEP = 256
FFN_STEPS = D_FF // FFN_STEP
EPS = 1e-6
NEG = -1e30
THETA = 500000.0
TRI = 384

Q_RANK, KV_RANK, ROPE = 384, 256, 32
MLA_IN = Q_RANK + KV_RANK + ROPE
MLA_QK = 64 + ROPE

DA_HEADS, DA_V = 4, 128
GLA_HEADS, GLA_DK, GLA_DV, GLA_RANK = 4, 32, 64, 16
GLA_TEMP = 16.0
SUB = 16
NSUB = P // SUB
IN_WIDTH = 3088

PK_HEADS, NKEYS, TOPK = 8, 128, 16
EXPERTS = NKEYS * NKEYS
PICKS = PK_HEADS * TOPK

GSLOTS, GCOLS = 4, 512
DSLOTS, DROWS = 2, 256
ROWSLOTS = GSLOTS * KT * GCOLS // D
NORMS = ("norm", "norm_ffn", "norm_final")
BURST = 16

FREQS = [16, ROPE, 16]
FREQ_AT = [0, 8, 24]
NFREQ = 32


class Phase:

    def __init__(self, kind, i=None, j=None, which=None, gain=None, last=None):
        self.kind, self.i, self.j, self.which, self.gain, self.last = kind, i, j, which, gain, last


def panels_of(kind):
    if kind == "sb":
        return [(512 * i, 512, "T" if i < 4 else "rows") for i in range(6)]
    if kind == "moba":
        return [(512 * i, 512, "rows") for i in range(6)]
    if kind == "mla_in":
        return [(0, 512, "rows"), (512, MLA_IN - 512, "rows")]
    if kind == "mla_uq":
        return [(512 * i, 512, "rows") for i in range(3)]
    if kind == "mla_ukv":
        return [(512 * i, 512, "rows") for i in range(4)]
    if kind == "pq":
        return [(512 * i, 512, "T") for i in range(4)]
    return [(0, 512, "rows"), (512, 512, "rows"), (1024, 512, "rows"), (1536, 512, "T"),
            (2048, 512, "T"), (2560, 512, "rows"), (3072, GLA_RANK, "narrow")]


RAISES = {
    "norm": dict(square_sum=2, mean_square=1, rstd=1, normed=2, turned=4, moved_even=2,
                 moved_odd=2, gains=1),
    "norm_ffn": dict(square_sum=2, mean_square=1, rstd=1, normed=2, turned=4, moved_even=2,
                     moved_odd=2, gains=1, x_hi=4),
    "norm_final": dict(square_sum=2, mean_square=1, rstd=1, normed=2, gains=1),
    "ffn": dict(wide=2 * FFN_STEPS, wide_read=2 * FFN_STEPS, silu=2 * FFN_STEPS,
                gated=2 * FFN_STEPS, hid_hi=2 * FFN_STEPS, deep=FFN_STEPS, resid=4, wide_hi=2 * FFN_STEPS,
                wide_lo=2 * FFN_STEPS, deep_hi=FFN_STEPS, deep_lo=FFN_STEPS),
    "sb": dict(wide=12, wide_read=12, deep=4, resid=4, scores=HEADS, masked=HEADS, log1p=HEADS,
               softplus=HEADS, tail=HEADS, tail_read=HEADS, weights=HEADS, mixed=HEADS,
               mixed_read=HEADS),
    "moba": dict(wide=12, wide_read=12, deep=4, resid=4, rotated=1, turned=8, moved_even=4,
                 moved_odd=4, scores=HEADS, masked=HEADS, row_max=HEADS, exps=HEADS,
                 probs=HEADS, probs_T=HEADS, weights=HEADS, mixed=HEADS, mixed_read=HEADS),
    "mla": dict(wide=18, wide_read=18, deep=4, resid=4, rotated=3, mean_square=1, rstd=1,
                turned=20, moved_even=10, moved_odd=10,
                scores=HEADS, masked=HEADS, row_max=HEADS, exps=HEADS,
                probs=HEADS, probs_T=HEADS, weights=HEADS, mixed=HEADS, mixed_read=HEADS),
    "mix2": dict(wide=14, wide_read=14, deep=4, resid=4, rotated=2, mean_square=2, rstd=2,
                 turned=8, moved_even=4, moved_odd=4,
                 scores=8, masked=8, row_max=8, exps=8, probs=8, probs_T=4, weights=4,
                 mixed=4, mixed_read=4),
    "peer": dict(wide=8, wide_read=8, turned=2, moved_even=1, moved_odd=1, key_scores=8,
                 key_scores_read=8, row_used=4 * PICKS),
}


def plan():
    phases = []
    for i in range(DEPTH):
        phases += [Phase("norm_ffn", gain=("norm_ffn1", i)), Phase("ffn", which=1, i=i),
                   Phase("norm", gain=("norm_mix", i)),
                   Phase(("sb", "moba", "mla")[i % 3], i=i, j=i // 3),
                   Phase("norm_ffn", gain=("norm_ffn2", i)), Phase("ffn", which=2, i=i)]
    phases.append(Phase("norm_final", gain=("final_norm", None), last=False))
    for i in range(DEPTH2):
        phases += [Phase("norm", gain=("norm_mix_2", i)), Phase("mix2", i=i),
                   Phase("norm", gain=("norm_ffn_2", i)), Phase("peer", i=i)]
    phases.append(Phase("norm_final", gain=("norm_final_2", None), last=True))
    total = {}
    for n, ph in enumerate(phases):
        ph.n = n
        ph.at = dict(total)
        for name, count in RAISES[ph.kind].items():
            total[name] = total.get(name, 0) + count
    return phases


def build(nc, A, out, stop=None):
    phases = plan()[:stop]
    ctx = ExitStack()
    with ctx:
        def sb(name, shape, dt=F32):
            return ctx.enter_context(nc.sbuf_tensor(name, shape, dt))

        def sem(name):
            return ctx.enter_context(nc.semaphore(name))

        wide_ring = sb("wide_ring", [P, GSLOTS, KT, GCOLS])
        deep_ring = sb("deep_ring", [P, DSLOTS, DROWS // P, D])
        row_ring = wide_ring[:].rearrange("p a b c -> p (a b c)").rearrange("p (n d) -> p n d", d=D)
        resid = sb("resid", [P, TT, D])
        xn = sb("xn", [P, TT, D])
        xT = sb("xT", [P, KT, TOK])
        gains = sb("gains", [P, 2, D])
        with ExitStack() as ffn_stage:
            def split(name, shape):
                return [ffn_stage.enter_context(nc.sbuf_tensor(f"{name}_{part}", shape, F32R))
                        for part in ("hi", "lo")]
            wide_hi, wide_lo = split("wide", [P, 2, KT, 2, P])
            deep_hi, deep_lo = split("deep", [P, DROWS // P, D])
            x_hi, x_lo = split("x", [P, KT, TOK])
            hid_hi, hid_lo = split("hid", [P, 4, TOK])
        arena = sb("arena", [P, 18432])

        def cut(at, *shape):
            n = int(np.prod(shape))
            assert at + n <= 18432, (at, shape)
            v = arena[:, at:at + n]
            names = " ".join("abcd"[:len(shape)])
            if len(shape) == 1:
                return v
            return v.rearrange(f"p ({names}) -> p {names}",
                               **{x: s for x, s in zip("abcd", shape)})

        silu_buf = xn[:, 0, 0:2 * TOK].rearrange("p (b t) -> p b t", b=2)
        hidden = xn[:, 0, 2 * TOK:4 * TOK].rearrange("p (b t) -> p b t", b=2)
        CORE = 16128
        core_a = cut(CORE, 2, TRI)
        core_b = cut(CORE + 768, 2, TRI)
        core_c = cut(CORE + 1536, 2, TRI)
        core_d = cut(CORE - 768, 2, TRI)
        core_e = cut(CORE - 1536, 2, TRI)
        sb_qT, sb_kT = cut(0, KT, TOK), cut(2048, KT, TOK)
        sb_v = cut(4096, TT, D)
        oT = cut(6144, KT, TOK)
        mo_qk = cut(8192, TT, 2 * D)
        mo_T = cut(0, 2 * KT, TOK)
        mo_v = cut(4096, TT, D)
        ml_T = cut(0, HEADS, 4 * P)
        ml_v = cut(8192, TT, D)
        ml_q = cut(10240, TT, HEADS, MLA_QK)
        ml_k = cut(13312, TT, HEADS, MLA_QK)
        ml_c = cut(16384, TT, MLA_IN)
        ml_oT = cut(10240, KT, TOK)
        ml_cT = xT[:, 0:5, :]
        m2_qk = cut(0, TT, 1024)
        m2_v = cut(2048, TT, DA_HEADS * DA_V)
        m2_sc = cut(3072, 6, TOK)
        m2_gq = cut(4608, 2, TOK)
        m2_gv = cut(5120, TT, 512)
        m2_lr = cut(6144, TOK)
        m2_b = cut(6400, TOK)
        m2_la = cut(6656, 3, TOK)
        m2_diag = cut(7424, 2, SUB, NSUB, SUB)
        m2_qkT = cut(7424, KT, TOK)
        m2_AT = cut(11520, 3, GLA_HEADS, P)
        m2_og = cut(13056, TT, 256)
        m2_od = cut(13568, TT, 512)
        m2_tmp = cut(14592, 2, 512)
        m2_mixT = xT
        m2_qsb = xn[:, 0, :].rearrange("p (n h i) -> p n h i", h=GLA_HEADS, i=SUB)
        m2_ks = xn[:, 1, :].rearrange("p (n t) -> p n t", t=TOK)
        pk_S = cut(0, TT, 16, NKEYS)
        pk_qT = cut(4096, 16, TOK)
        pk_cand = cut(8192, 256)
        pk_v = cut(8448, 16, TOPK)
        pk_i = cut(8704, 16, TOPK).bitcast(U32)
        pk_if = cut(8960, 16, TOPK)
        pk_hot = cut(9216, PK_HEADS * TOPK, TOPK)
        pk_sc = cut(11264, PK_HEADS, TOPK)
        pk_ci = cut(11392, PK_HEADS, TOPK).bitcast(U32)
        pk_ab = cut(11520, 2, PICKS)
        pk_abu = cut(11776, 2, PICKS).bitcast(U32)
        pk_e = cut(12032, 2, PICKS)
        pk_gate = cut(12288, TT, PICKS)
        pk_dot = cut(12544, PICKS)
        pk_coef = cut(12672, PICKS)
        pk_idx = cut(12800, TT, PICKS).bitcast(U32)
        pk_burst = cut(13056, 2, BURST).bitcast(U32)
        pk_dots = cut(13088, 2, BURST)
        pk_den = cut(13120, PK_HEADS)
        pk_scratch = cut(13312, D)
        pk_keys = cut(14336, 2, PEER_D := P)
        pk_keysT = cut(14592, 2, P)

        ident = sb("ident", [P, P])
        ones = sb("ones", [P, P])
        later = sb("later", [P, P])
        mask_T = sb("mask_T", [P, TRI])
        mask_rows = sb("mask_rows", [P, TRI])
        head_of = sb("head_of", [P, GLA_HEADS])
        earlier_sub = sb("earlier_sub", [P, NSUB])
        same_sub = sb("same_sub", [P, NSUB, SUB])
        iota16 = sb("iota16", [P, TOPK])
        minus_half = sb("minus_half", [P, 16])
        zeros_tok = sb("zeros_tok", [P, TOK])
        trig = sb("trig", [P, 2, TT, NFREQ])
        ang = sb("ang", [P, 4, TT, NFREQ])
        inv_freq = sb("inv_freq", [P, NFREQ])
        posf = sb("posf", [P, 2, TT])
        posi = sb("posi", [P, TT], I32)
        small = sb("small", [P, 64])
        mla_gain = sb("mla_gain", [P, Q_RANK + KV_RANK])
        diff_gain = sb("diff_gain", [P, DEPTH2, DA_V])
        gla_gain = sb("gla_gain", [P, DEPTH2, GLA_DV])
        lam_rows = sb("lam_rows", [P, DEPTH2, 4, 64])
        minus_lam = sb("minus_lam", [P, DEPTH2])
        conv_taps = sb("conv_taps", [P, DEPTH2, 2, 3])
        gate2 = sb("gate2", [GLA_RANK, DEPTH2, P])
        gate_bias = sb("gate_bias", [P, DEPTH2])

        bank = [ctx.enter_context(nc.psum_tensor(f"bank{i}", [P, 512], F32)) for i in range(8)]
        acc = [[bank[0], bank[1]], [bank[2], bank[3]]]
        work = bank[4:8]

        S = {name: sem(name) for name in (
            "square_sum",
            "mean_square",
            "rstd",
            "normed",
            "turned",
            "moved_even",
            "moved_odd",
            "x_hi",
            "wide_hi",
            "wide_lo",
            "deep_hi",
            "deep_lo",
            "gated", "hid_hi",
            "wide",
            "wide_read",
            "silu",
            "deep",
            "resid",
            "scores",
            "masked",
            "log1p",
            "softplus",
            "tail",
            "tail_read",
            "row_max",
            "exps",
            "probs",
            "probs_T",
            "weights",
            "mixed",
            "mixed_read",
            "rotated",
            "key_scores",
            "key_scores_read",
            "row_used",
            "picked",
            "dots_moved",
            "row_asked",
            "numbers",
            "gelu",
            "gate_exp_in", "gate_exp",
            "decay_x", "decay_l",
            "gate_mm",
            "running",
            "diag_in", "diag_exp", "diag_ready", "diag_mm",
            "qs_in", "qs_exp", "qs_ready",
            "ks_in", "ks_exp", "ks_ready", "off_mm",
            "att_ready", "gla_mm", "gla_read", "out_gate",
            "conv_done",
            "dve_chain", "act_chain", "pool_chain",
            "consts",
            "trig_in", "trig", "lam_in", "lam_exp",
            "params", "keys_in", "stored")}
        wide_in = [sem(f"wide_in{i}") for i in range(GSLOTS)]
        deep_in = [sem(f"deep_in{i}") for i in range(DSLOTS)]
        gain_in = [sem(f"gain_in{i}") for i in range(2)]
        row_in = [sem(f"row_in{i}") for i in range(ROWSLOTS)]

        def seen(count):
            return max(count, 0)

        class Chain:

            def __init__(self, eng, name):
                self.eng, self.name, self.n = eng, name, 0

            def __call__(self, ins):
                self.n += 1
                ins.then_inc(S[self.name], 1)
                self.eng.wait_ge(S[self.name], self.n)

        def halves(panel):
            v = panel.rearrange("p k (u j m) -> p k u j m", u=2, j=2)
            return [v[:, :, :, j] for j in range(2)]

        def ds(at, n):
            return bass.ds(at, n)

        def panels(ph):
            def of(kind, w, kt, src):
                return [(w, kt, src, c0, n, lay) for c0, n, lay in panels_of(kind)]
            if ph.kind == "sb":
                return of("sb", A["sb_w_qkv"][ph.j], KT, xT)
            if ph.kind == "moba":
                return of("moba", A["moba_w_qkv"][ph.j], KT, xT)
            if ph.kind == "mla":
                return (of("mla_in", A["mla_w_in"][ph.j], KT, xT)
                        + of("mla_uq", A["mla_w_uq"][ph.j], 3, ml_cT[:, 0:3])
                        + of("mla_ukv", A["mla_w_ukv"][ph.j], 2, ml_cT[:, 3:5]))
            if ph.kind == "mix2":
                return of("mix2", A["w_in_2"][ph.i], KT, xT)
            if ph.kind == "peer":
                return of("pq", A["peer_w_q_2"][ph.i], KT, xT)
            return []

        def out_weights(ph):
            return {"sb": lambda: A["sb_w_o"][ph.j], "moba": lambda: A["moba_w_o"][ph.j],
                    "mla": lambda: A["mla_w_o"][ph.j], "mix2": lambda: A["w_out_2"][ph.i]}[ph.kind]()

        mo_groups = [[mo_qk[:, t, c * P:(c + 1) * P] for c in (2 * g, 2 * g + 1) for t in range(TT)]
                     for g in range(KT)]
        ml_c_groups = [[ml_c[:, t, c * P:(c + 1) * P] for c in cs for t in range(TT)]
                       for cs in ((0,), (1,), (2,), (3, 4))]
        ml_groups = [[m[:, t, h] for m in (ml_q, ml_k) for t in range(TT)] for h in range(HEADS)]
        m2_qk_groups = [[m2_qk[:, t, c * P:(c + 1) * P] for c in (2 * g, 2 * g + 1)
                         for t in range(TT)] for g in range(4)]
        m2_out_groups = ([[m2_od[:, t, c * P:(c + 1) * P] for c in (2 * g, 2 * g + 1)
                           for t in range(TT)] for g in range(2)]
                         + [[m2_og[:, t, c * P:(c + 1) * P] for t in range(TT)] for c in range(2)])
        pk_groups = [[pk_keys[:, m]] for m in range(2)]

        def turned_to(ph, g):
            if ph.kind in ("norm", "norm_ffn"):
                t, half = g // 2, g % 2
                return P, xT[:, 4 * half:4 * half + 4, t * P:(t + 1) * P], 512
            if ph.kind == "moba":
                return P, mo_T[:, 2 * g:2 * g + 2].rearrange("p c t -> p (c t)"), 512
            if ph.kind == "mla":
                if g < 4:
                    n = 1 + (g == 3)
                    return P, ml_cT[:, g:g + n].rearrange("p c t -> p (c t)"), n * TOK
                return MLA_QK, ml_T[0:MLA_QK, g - 4], 512
            if ph.kind == "mix2":
                if g < 4:
                    return P, m2_qkT[:, 2 * g:2 * g + 2].rearrange("p c t -> p (c t)"), 512
                c, n = ((0, 2), (2, 2), (6, 1), (7, 1))[g - 4]
                return P, m2_mixT[:, c:c + n].rearrange("p c t -> p (c t)"), n * TOK
            return P, pk_keysT[:, g], P

        def move_turned(eng, ph, groups, op, name):
            for g in groups:
                n = ph.at.get("turned", 0) + g
                if n % 2 != (0 if name == "moved_even" else 1):
                    continue
                parts, dst, cols = turned_to(ph, g)
                eng.wait_ge(S["turned"], seen(n + 1))
                src = work[n % 4][0:parts, 0:cols]
                if len(dst.shape) == 3:
                    src = src.rearrange("p (a b) -> p a b", a=dst.shape[1])
                op(dst, src).then_inc(S[name], 1)

        wide_dmas, n = [], [0] * GSLOTS
        for ph in phases:
            for k in range(RAISES[ph.kind].get("wide", 0) // 2):
                g = ph.at.get("wide", 0) // 2 + k
                n[g % GSLOTS] += 2 if ph.kind == "ffn" else 1
                wide_dmas.append(n[g % GSLOTS])

        def wait_resid(eng, ph):
            eng.wait_ge(S["params"], 16 * N_PARAMS)
            eng.wait_ge(S["resid"], ph.at.get("resid", 0))
            eng.wait_ge(S["normed"], ph.at.get("normed", 0))
            eng.wait_ge(S["row_used"], ph.at.get("row_used", 0))

        N_PARAMS = 4 + DEPTH2 * 9 + 1

        block = ctx.enter_context(nc.Block())

        @block.sync
        def _(sp):
            def load_wide(ph, k, dst_src):
                g = ph.at.get("wide", 0) // 2
                slot = (g + (k if isinstance(k, int) else k[1])) % GSLOTS
                n = k if isinstance(k, int) else k[0]
                sp.wait_ge(S["wide"], seen(ph.at.get("wide", 0) + 2 * (n - GSLOTS + 1)))
                for dst, src in dst_src(slot):
                    sp.dma_start(dst, src).then_inc(wide_in[slot], 16)

            def load_deep(ph, k, w):
                d = ph.at.get("deep", 0)
                slot = (d + (k if isinstance(k, int) else k[1])) % DSLOTS
                n = k if isinstance(k, int) else k[0]
                sp.wait_ge(S["deep"], seen(d + n - DSLOTS + 1))
                src = w.rearrange("(s c p) n -> s p c n", p=P, c=DROWS // P)
                sp.dma_start(deep_ring[:, slot], src[n] if isinstance(n, int) else
                             src[ds(n, 1)].rearrange("s p c n -> (s p) c n")).then_inc(deep_in[slot], 16)

            for ph in phases:
                if ph.kind == "ffn":
                    up = A[f"ffn{ph.which}_w_gate_up"][ph.i].rearrange(
                        "(k p) (u n) -> p k u n", p=P, u=2)
                    down = A[f"ffn{ph.which}_w_down"][ph.i]

                    def gate_up(n):
                        def both(slot):
                            dst = wide_ring[:, slot].rearrange("p k (u n) -> p k u n", u=2)
                            return [(dst[:, :, u], up[:, :, u, ds(n * FFN_STEP, FFN_STEP)])
                                    for u in range(2)]
                        return both

                    def step(n, s):
                        load_wide(ph, (n, s), gate_up(n))
                        load_deep(ph, (n, s), down)

                    head = 4 if ph.at.get("wide", 0) == 0 else 3
                    for s in range(head):
                        step(s, s)
                    if head == 3:
                        with sp.Fori(0, 2) as r:
                            for s in range(3, 7):
                                step(r * 4 + s, s)
                    else:
                        for s in range(head, FFN_STEPS):
                            step(s, s)
                elif ph.kind in ("sb", "moba", "mla", "mix2", "peer"):
                    if ph.kind == "mix2" and ph.i > 0:
                        sp.wait_ge(S["row_used"], ph.at["row_used"])
                    for k, (w, kt, _, c0, n, _) in enumerate(panels(ph)):
                        def cols(slot, w=w, kt=kt, c0=c0, n=n):
                            return [(wide_ring[:, slot, 0:kt, 0:n],
                                     w.rearrange("(k p) n -> p k n", p=P)[:, :, c0:c0 + n])]
                        load_wide(ph, k, cols)
                    if ph.kind != "peer":
                        for k in range(4):
                            load_deep(ph, k, out_weights(ph))
            last = phases[-1]
            if last.kind == "norm_final":
                sp.wait_ge(S["normed"], last.at["normed"] + 2)
                src = xn
            else:
                sp.wait_ge(S["resid"], last.at.get("resid", 0) + RAISES[last.kind].get("resid", 0))
                src = resid
            sp.dma_start(out[0].rearrange("(t p) d -> p t d", p=P), src[:]).then_inc(S["stored"], 16)
            sp.wait_ge(S["stored"], 16)

        @block.tensor
        def _(pe):
            mm = nc.tensor.matmul

            def await_wide(ph, k):
                g = ph.at.get("wide", 0) // 2 + k
                need = 16 * wide_dmas[g]
                pe.wait_ge(wide_in[g % GSLOTS], need)

            def await_deep(ph, k):
                d = ph.at.get("deep", 0) + k
                need = 16 * (d // DSLOTS + 1)
                pe.wait_ge(deep_in[d % DSLOTS], need)

            def wide_products(ph):
                for k, (_, kt, src, c0, n, layout) in enumerate(panels(ph)):
                    if ph.kind == "mla" and k == 2:
                        pe.wait_ge(S["rotated"], ph.at["rotated"] + 1)
                        turn_groups(ph, 0, ml_c_groups)
                        pe.wait_ge(S["moved_even"], ph.at["moved_even"] + 2)
                        pe.wait_ge(S["moved_odd"], ph.at["moved_odd"] + 2)
                    slot = (ph.at["wide"] // 2 + k) % GSLOTS
                    await_wide(ph, k)
                    for j in range(2):
                        t = ph.at["wide"] + 2 * k + j
                        pe.wait_ge(S["wide_read"], seen(t - 3))
                        b, w = work[t % 4], wide_ring[:, slot]
                        if layout == "rows":
                            for c in range(kt):
                                ins = mm(b[:, 0:n], src[:, c, j * P:(j + 1) * P], w[:, c, 0:n],
                                         start=c == 0, stop=c == kt - 1)
                        elif layout == "T":
                            for i in range(2):
                                m = (2 * j + i) * P
                                for c in range(kt):
                                    ins = mm(b[:, i * TOK:(i + 1) * TOK], w[:, c, m:m + P], src[:, c, :],
                                             start=c == 0, stop=c == kt - 1)
                        else:
                            for c in range(kt):
                                ins = mm(b[0:n, 0:P], w[:, c, 0:n], src[:, c, j * P:(j + 1) * P],
                                         start=c == 0, stop=c == kt - 1)
                        ins.then_inc(S["wide"], 1)

            def deep_product(ph, k, last, lhs):
                await_deep(ph, k)
                w = deep_ring[:, (ph.at.get("deep", 0) + k) % DSLOTS]
                for c in range(2):
                    for t in range(TT):
                        for h in range(2):
                            ins = mm(acc[t][h][:, :], lhs(c)[:, t * P:(t + 1) * P],
                                     w[:, c, h * 512:(h + 1) * 512],
                                     start=k == 0 and c == 0,
                                     stop=last and c == 1, skip_group_check=True)
                ins.then_inc(S["deep"], 1)

            def turn_groups(ph, first, groups):
                for g, tiles in enumerate(groups):
                    n = ph.at["turned"] + first + g
                    pe.wait_ge(S["moved_even" if n % 2 == 0 else "moved_odd"], seen((n - 4) // 2 + 1))
                    for i, src in enumerate(tiles):
                        ins = nc.tensor.transpose(work[n % 4][0:src.shape[1], i * P:(i + 1) * P],
                                                  src, ident[:])
                    ins.then_inc(S["turned"], 1)

            def norm(ph):
                for t in range(TT):
                    pe.wait_ge(S["normed"], ph.at.get("normed", 0) + t + 1)
                    for half in range(2):
                        g = ph.at.get("turned", 0) + 2 * t + half
                        pe.wait_ge(S["moved_even" if g % 2 == 0 else "moved_odd"], seen((g - 4) // 2 + 1))
                        for i in range(4):
                            c = 4 * half + i
                            ins = nc.tensor.transpose(work[g % 4][:, i * P:(i + 1) * P],
                                                      xn[:, t, c * P:(c + 1) * P], ident[:])
                        ins.then_inc(S["turned"], 1)
                pe.wait_ge(S["moved_even"], ph.at.get("moved_even", 0) + 2)
                pe.wait_ge(S["moved_odd"], ph.at.get("moved_odd", 0) + 2)

            def ffn(ph):
                at = ph.at

                def split_mm(o, w, x, start, stop):
                    mm(o, w[0], x[0], start=start, stop=False, skip_group_check=True)
                    mm(o, w[0], x[1], start=False, stop=False, skip_group_check=True)
                    return mm(o, w[1], x[0], start=False, stop=stop, skip_group_check=True)

                def gate_up(s, r=None):
                    for j in range(2):
                        n = at.get("wide_lo", 0) + 2 * s + j + 1
                        pe.wait_ge(S["wide_lo"], n if r is None else r * 8 + n)
                        t = at.get("wide", 0) + 2 * s + j
                        if r is None:
                            pe.wait_ge(S["wide_read"], seen(t - 3))
                        else:
                            pe.wait_ge(S["wide_read"], r * 8 + (t - 3))
                        for u in range(2):
                            for k in range(KT):
                                ins = split_mm(work[t % 4][:, u * TOK:(u + 1) * TOK],
                                               [w[:, j, k, u] for w in (wide_hi, wide_lo)],
                                               [x[:, k] for x in (x_hi, x_lo)],
                                               k == 0, k == KT - 1)
                        ins.then_inc(S["wide"], 1)

                def down(s, r=None):
                    need = at.get("wide", 0) + 2 * (s + 1)
                    pe.wait_ge(S["wide_read"], need if r is None else r * 8 + need)
                    need = at.get("deep_lo", 0) + s + 1
                    pe.wait_ge(S["deep_lo"], need if r is None else r * 4 + need)
                    t0 = at.get("wide", 0) + 2 * s
                    for c in range(2):
                        for t in range(TT):
                            for h in range(2):
                                ins = split_mm(acc[t][h][:, :],
                                               [x[:, (t0 + c) % 4, t * P:(t + 1) * P]
                                                for x in (hid_hi, hid_lo)],
                                               [w[:, c, h * 512:(h + 1) * 512]
                                                for w in (deep_hi, deep_lo)],
                                               s == 0 and c == 0 and r is None,
                                               s == FFN_STEPS - 1 and c == 1)
                    ins.then_inc(S["deep"], 1)

                for s in range(3):
                    gate_up(s)
                    if s:
                        down(s - 1)
                with pe.Fori(0, 2) as r:
                    for s in range(3, 7):
                        gate_up(s, r)
                        down(s - 1, r)
                down(FFN_STEPS - 1)

            def out_product(ph, k, src):
                deep_product(ph, k, k == 3, lambda c: src[:, 2 * k + c, :])

            def stick_breaking(ph):
                wide_products(ph)
                pe.wait_ge(S["wide_read"], ph.at["wide_read"] + 12)
                at = ph.at

                def scores(h):
                    pe.wait_ge(S["masked"], seen(at.get("masked", 0) + h - 1))
                    p0, c = HD * (h % 2), h // 2
                    q, k = sb_qT[p0:p0 + HD, c], sb_kT[p0:p0 + HD, c]
                    mm(work[h % 2][:, 0:TOK], k[:, 0:P], q, start=True, stop=True)
                    mm(work[h % 2][:, TOK:TRI], k[:, P:TOK], q[:, P:TOK], start=True,
                       stop=True).then_inc(S["scores"], 1)

                def tails(h):
                    pe.wait_ge(S["softplus"], at.get("softplus", 0) + h + 1)
                    pe.wait_ge(S["tail_read"], at.get("tail_read", 0) + h)
                    sp_ = core_c[:, h % 2]
                    mm(work[2][:, 0:P], later[:], sp_[:, 0:P], start=True, stop=True)
                    mm(work[2][:, P:TOK], later[:], sp_[:, P:TOK], start=True, stop=False,
                       skip_group_check=True)
                    mm(work[2][:, P:TOK], ones[:], sp_[:, TOK:TRI], start=False, stop=True,
                       skip_group_check=True)
                    mm(work[2][:, TOK:TRI], later[:], sp_[:, TOK:TRI], start=True, stop=True,
                       skip_group_check=True).then_inc(S["tail"], 1)

                for i in range(HEADS + 3):
                    if i < HEADS:
                        scores(i)
                    if 0 <= i - 1 < HEADS:
                        tails(i - 1)
                    if 0 <= i - 2 < HEADS:
                        mix_values(ph, i - 2, sb_v, core_e)
                    if i >= 6 and (i - 6) % 4 == 0:
                        pe.wait_ge(S["mixed_read"], seen(at.get("mixed_read", 0) + i - 2))
                        out_product(ph, (i - 6) // 4, oT)

            def mix_values(ph, h, v, w):
                pe.wait_ge(S["weights"], ph.at.get("weights", 0) + h + 1)
                pe.wait_ge(S["mixed_read"], ph.at.get("mixed_read", 0) + h)
                o, w, c = work[3][:, (h % 2) * TOK:(h % 2 + 1) * TOK], w[:, h % 2], (h // 2) * P
                mm(o[:, 0:P], v[:, 0, c:c + P], w[:, 0:P], start=True, stop=True, skip_group_check=True)
                mm(o[:, P:TOK], v[:, 0, c:c + P], w[:, P:TOK], start=True, stop=False,
                   skip_group_check=True)
                mm(o[:, P:TOK], v[:, 1, c:c + P], w[:, TOK:TRI], start=False, stop=True,
                   skip_group_check=True).then_inc(S["mixed"], 1)

            def soft_scores(ph, u, q, k):
                pe.wait_ge(S["masked"], seen(ph.at.get("masked", 0) + u - 1))
                mm(work[u % 2][:, 0:P], q[:, 0:P], k[:, 0:P], start=True, stop=True)
                mm(work[u % 2][:, P:TRI], q[:, P:TOK], k, start=True, stop=True).then_inc(S["scores"], 1)

            def turn_probs(ph, u, n):
                pe.wait_ge(S["probs"], ph.at.get("probs", 0) + u + 1)
                pe.wait_ge(S["weights"], ph.at.get("weights", 0) + n)
                for i in range(3):
                    ins = nc.tensor.transpose(work[2][:, i * P:(i + 1) * P],
                                              core_b[:, u % 2, i * P:(i + 1) * P], ident[:])
                ins.then_inc(S["probs_T"], 1)

            def softmax_heads(ph, qk, v, o):
                for i in range(HEADS + 3):
                    if i < HEADS:
                        soft_scores(ph, i, *qk(i))
                    if 0 <= i - 1 < HEADS:
                        turn_probs(ph, i - 1, i - 1)
                    if 0 <= i - 2 < HEADS:
                        mix_values(ph, i - 2, v, core_c)
                    if i >= 6 and (i - 6) % 4 == 0:
                        pe.wait_ge(S["mixed_read"], seen(ph.at.get("mixed_read", 0) + i - 2))
                        out_product(ph, (i - 6) // 4, o)

            def block_attention(ph):
                wide_products(ph)
                pe.wait_ge(S["rotated"], ph.at.get("rotated", 0) + 1)
                pe.wait_ge(S["wide_read"], ph.at["wide_read"] + 12)
                turn_groups(ph, 0, mo_groups)
                pe.wait_ge(S["moved_even"], ph.at["moved_even"] + 4)
                pe.wait_ge(S["moved_odd"], ph.at["moved_odd"] + 4)

                def qk(h):
                    p0, c = HD * (h % 2), h // 2
                    return mo_T[p0:p0 + HD, c], mo_T[p0:p0 + HD, KT + c]
                softmax_heads(ph, qk, mo_v, oT)

            def latent_attention(ph):
                wide_products(ph)
                pe.wait_ge(S["rotated"], ph.at["rotated"] + 3)
                pe.wait_ge(S["wide_read"], ph.at["wide_read"] + 18)
                turn_groups(ph, 4, ml_groups)
                pe.wait_ge(S["moved_even"], ph.at["moved_even"] + 10)
                pe.wait_ge(S["moved_odd"], ph.at["moved_odd"] + 10)

                def qk(h):
                    return ml_T[0:MLA_QK, h, 0:TOK], ml_T[0:MLA_QK, h, TOK:2 * TOK]
                softmax_heads(ph, qk, ml_v, ml_oT)

            def parallel_mixer(ph):
                at = ph.at
                i = ph.i
                wide_products(ph)
                pe.wait_ge(S["wide_read"], at["wide_read"] + 14)
                mm(work[0][:, 0:TOK], gate2[:, i], m2_lr[0:GLA_RANK], start=True,
                   stop=True).then_inc(S["gate_mm"], 1)
                for t in range(TT):
                    pe.wait_ge(S["diag_ready"], 2 * i + t + 1)
                    for ii in range(SUB):
                        ins = mm(work[1][:, (t * SUB + ii) * 4:(t * SUB + ii) * 4 + 4],
                                 m2_diag[:, t, ii].rearrange("p n j -> p (n j)"), head_of[:],
                                 start=True, stop=True, skip_group_check=True)
                    ins.then_inc(S["diag_mm"], 1)
                pe.wait_ge(S["qs_ready"], i + 1)
                for n in range(1, 2 * NSUB):
                    pe.wait_ge(S["ks_ready"], seen(15 * i + n))
                    slot = (n + 15 * i) % 4
                    q = m2_qsb[:, n].rearrange("p h i -> p (h i)")
                    at_n = (n % NSUB) * 64
                    ins = mm(work[2 + n // NSUB][:, at_n:at_n + 64], m2_ks[:, slot, 0:P], q,
                             start=True, stop=True, skip_group_check=True)
                    if n > NSUB:
                        ins = mm(bank[0][:, at_n:at_n + 64], m2_ks[:, slot, P:TOK], q,
                                 start=True, stop=True, skip_group_check=True)
                    ins.then_inc(S["off_mm"], 1)
                pe.wait_ge(S["att_ready"], i + 1)
                for t in range(TT):
                    for h in range(GLA_HEADS):
                        o = bank[1][:, t * 256 + h * 64:t * 256 + h * 64 + 64]
                        for kt in range(t + 1):
                            ins = mm(o, m2_AT[:, 0 if t == 0 else 1 + kt, h],
                                     m2_gv[:, kt, h * 64:h * 64 + 64], start=kt == 0, stop=kt == t,
                                     skip_group_check=True)
                ins.then_inc(S["gla_mm"], 1)
                pe.wait_ge(S["rotated"], at["rotated"] + 1)
                turn_groups(ph, 0, m2_qk_groups)
                pe.wait_ge(S["moved_even"], at["moved_even"] + 2)
                pe.wait_ge(S["moved_odd"], at["moved_odd"] + 2)
                for u in range(2 * DA_HEADS + 3):
                    if u < 2 * DA_HEADS:
                        p0, c = 64 * (u % 2), u // 2
                        soft_scores(ph, u, m2_qkT[p0:p0 + 64, c], m2_qkT[p0:p0 + 64, 4 + c])
                    if u >= 2 and u % 2 == 0 and u // 2 <= DA_HEADS:
                        turn_probs(ph, u - 1, u // 2 - 1)
                    if u >= 3 and u % 2 == 1:
                        h = (u - 3) // 2
                        pe.wait_ge(S["weights"], at.get("weights", 0) + h + 1)
                        pe.wait_ge(S["mixed_read"], at.get("mixed_read", 0) + h)
                        o, w = work[3][:, (h % 2) * 256:(h % 2) * 256 + 256], core_c[:, h % 2]
                        v = m2_v[:, :, h * DA_V:(h + 1) * DA_V]
                        mm(o[:, 0:P], w[:, 0:P], v[:, 0], start=True, stop=True, skip_group_check=True)
                        mm(o[:, P:256], w[:, P:TOK], v[:, 0], start=True, stop=False,
                           skip_group_check=True)
                        mm(o[:, P:256], w[:, TOK:TRI], v[:, 1], start=False, stop=True,
                           skip_group_check=True).then_inc(S["mixed"], 1)
                pe.wait_ge(S["rotated"], at["rotated"] + 2)
                turn_groups(ph, 4, m2_out_groups)
                pe.wait_ge(S["moved_even"], at["moved_even"] + 4)
                pe.wait_ge(S["moved_odd"], at["moved_odd"] + 4)
                pe.wait_ge(S["conv_done"], i + 1)
                for k in range(4):
                    out_product(ph, k, m2_mixT)

            def product_keys(ph):
                wide_products(ph)
                pe.wait_ge(S["keys_in"], 32 * (ph.i + 1))
                pe.wait_ge(S["wide_read"], ph.at["wide_read"] + 8)
                turn_groups(ph, 0, pk_groups)
                pe.wait_ge(S["moved_even"], ph.at["moved_even"] + 1)
                pe.wait_ge(S["moved_odd"], ph.at["moved_odd"] + 1)
                for n in range(8):
                    t, g = n // 4, n % 4
                    pe.wait_ge(S["key_scores_read"], seen(8 * ph.i + n - 3 if n > 3 else 0))
                    for i in range(4):
                        c = 4 * g + i
                        ins = mm(work[n % 4][:, i * P:(i + 1) * P], pk_qT[:, c, t * P:(t + 1) * P],
                                 pk_keysT[:, c % 2], start=True, stop=True, skip_group_check=True)
                    ins.then_inc(S["key_scores"], 1)

            pe.wait_ge(S["consts"], 1)
            for ph in phases:
                {"norm": norm, "norm_ffn": norm, "norm_final": lambda ph: None, "ffn": ffn, "sb": stick_breaking,
                 "moba": block_attention, "mla": latent_attention, "mix2": parallel_mixer,
                 "peer": product_keys}[ph.kind](ph)

        @block.scalar
        def _(act):
            chain = Chain(act, "act_chain")
            A_ = nc.scalar.activation

            def move(dst, src):
                return A_(dst, src, ACT.Copy)

            def rows(ap):
                return ap.partition_broadcast(P)
            n = [0]

            def param(dst, src):
                act.dma_start(dst, src, allow_slow_non_contiguous=True).then_inc(S["params"], 16)
                n[0] += 16
            act.dma_start(resid[:], A["x"][0].rearrange("(t p) d -> p t d", p=P)).then_inc(S["params"], 16)
            param(posi[:], A["positions_2"].rearrange("a (t p) -> p (a t)", p=P))
            param(mla_gain[:, 0:Q_RANK], rows(A["mla_q_norm"][0]))
            param(mla_gain[:, Q_RANK:], rows(A["mla_kv_norm"][0]))
            for i in range(DEPTH2):
                param(diff_gain[:, i], rows(A["diff_norm_2"][i]))
                param(gla_gain[:, i], rows(A["gla_norm_2"][i]))
                for m, nm in enumerate(("lam_q1_2", "lam_k1_2", "lam_q2_2", "lam_k2_2")):
                    param(lam_rows[:, i, m], rows(A[nm][i]))
                param(gate2[:, i], A["gla_w_gate2_2"][i])
                for c in range(2):
                    param(conv_taps[:, i, c], A["conv_w_2"][i].rearrange("j (c p) -> c p j", p=P)[c])
            param(gate_bias[:], A["gla_b_gate_2"].rearrange("l p -> p l"))

            def norm(ph):
                wait_resid(act, ph)
                for t in range(TT):
                    act.wait_ge(S["normed"], ph.at.get("normed", 0))
                    A_(xn[:, t], resid[:, t], ACT.Square,
                       accum_out=small[:, t:t + 1]).then_inc(S["square_sum"], 1)
                if ph.kind == "norm":
                    move_turned(act, ph, range(4), move, "moved_even")
                elif ph.kind == "norm_ffn":
                    ffn_phase = phases[ph.n + 1] if ph.n + 1 < len(phases) else None
                    if ffn_phase:
                        wide_half(ffn_phase, 0, 0)
                        wide_half(ffn_phase, 0, 1)
                    for g in range(4):
                        n = ph.at.get("turned", 0) + g
                        act.wait_ge(S["turned"], n + 1)
                        t, half = g // 2, g % 2
                        A_(x_hi[:, 4 * half:4 * half + 4, t * P:(t + 1) * P],
                           work[n % 4][:, :].rearrange("p (a b) -> p a b", a=4),
                           ACT.Copy).then_inc(S["x_hi"], 1)

            def wide_half(ph, s, j, r=None):
                g = ph.at.get("wide", 0) // 2 + s
                need = 16 * wide_dmas[g]
                act.wait_ge(wide_in[g % GSLOTS], need if r is None else r * 32 + need)
                need = ph.at.get("wide", 0) + 2 * (s - 1) + j + 1
                if r is None:
                    act.wait_ge(S["wide"], seen(need))
                else:
                    act.wait_ge(S["wide"], r * 8 + need)
                A_(wide_hi[:, j], halves(wide_ring[:, g % GSLOTS])[j],
                   ACT.Copy).then_inc(S["wide_hi"], 1)

            def ffn(ph):
                at = ph.at

                def silu(s, j, r=None):
                    n = at.get("wide", 0) + 2 * s + j
                    if r is None:
                        act.wait_ge(S["wide"], n + 1)
                        act.wait_ge(S["wide_read"], seen(n - 1))
                    else:
                        act.wait_ge(S["wide"], r * 8 + (n + 1))
                        act.wait_ge(S["wide_read"], r * 8 + (n - 1))
                    A_(silu_buf[:, n % 2], work[n % 4][:, 0:TOK], ACT.Silu).then_inc(S["silu"], 1)

                def deep_panel(s, r=None):
                    d = at.get("deep", 0) + s
                    need = 16 * (d // DSLOTS + 1)
                    act.wait_ge(deep_in[d % DSLOTS], need if r is None else r * 32 + need)
                    if r is None:
                        act.wait_ge(S["deep"], d)
                    else:
                        act.wait_ge(S["deep"], r * 4 + d)
                    A_(deep_hi[:], deep_ring[:, d % DSLOTS], ACT.Copy).then_inc(S["deep_hi"], 1)

                def step(s, r=None):
                    for j in range(2):
                        silu(s - 1, j, r)
                        wide_half(ph, s, j, r)
                    deep_panel(s - 1, r)
                step(1)
                step(2)
                with act.Fori(0, 2) as r:
                    for s in range(3, 7):
                        step(s, r)
                silu(FFN_STEPS - 1, 0)
                silu(FFN_STEPS - 1, 1)
                deep_panel(FFN_STEPS - 1)

            def stick_breaking(ph):
                at = ph.at
                for i in range(HEADS + 1):
                    if i < HEADS:
                        act.wait_ge(S["masked"], at.get("masked", 0) + i + 1)
                        act.wait_ge(S["softplus"], seen(at.get("softplus", 0) + i - 1))
                        l = core_b[:, i % 2]
                        chain(A_(l, core_a[:, i % 2], ACT.Abs))
                        chain(A_(l, l, ACT.Exp, scale=-1.0))
                        A_(l, l, ACT.Ln, bias=1.0).then_inc(S["log1p"], 1)
                    if i >= 1:
                        h = i - 1
                        act.wait_ge(S["tail_read"], at.get("tail_read", 0) + h + 1)
                        act.wait_ge(S["mixed"], seen(at.get("mixed", 0) + h - 1))
                        A_(core_e[:, h % 2], core_d[:, h % 2], ACT.Exp).then_inc(S["weights"], 1)

            def soft_exp(ph, u):
                act.wait_ge(S["row_max"], ph.at.get("row_max", 0) + u + 1)
                e, s = core_b[:, u % 2], core_a[:, u % 2]
                act.wait_ge(S["probs"], seen(ph.at.get("probs", 0) + u - 1))
                A_(e[:, 0:P], s[:, 0:P], ACT.Exp, bias=small[:, 8 + 2 * (u % 2):9 + 2 * (u % 2)],
                   accum_out=small[:, 12 + 2 * (u % 2):13 + 2 * (u % 2)])
                A_(e[:, P:TRI], s[:, P:TRI], ACT.Exp, bias=small[:, 9 + 2 * (u % 2):10 + 2 * (u % 2)],
                   accum_out=small[:, 13 + 2 * (u % 2):14 + 2 * (u % 2)]).then_inc(S["exps"], 1)

            def move_probs(ph, h):
                act.wait_ge(S["probs_T"], ph.at.get("probs_T", 0) + h + 1)
                act.wait_ge(S["mixed"], seen(ph.at.get("mixed", 0) + h - 1))
                A_(core_c[:, h % 2], work[2][:, 0:TRI], ACT.Copy).then_inc(S["weights"], 1)

            def softmax_heads(ph):
                for i in range(HEADS + 1):
                    if i < HEADS:
                        act.wait_ge(S["probs_T"], seen(ph.at.get("probs_T", 0) + i - 1))
                        soft_exp(ph, i)
                    if i >= 1:
                        move_probs(ph, i - 1)

            def block_attention(ph):
                move_turned(act, ph, range(8), move, "moved_even")
                softmax_heads(ph)

            def latent_attention(ph):
                move_turned(act, ph, range(20), move, "moved_even")
                softmax_heads(ph)

            def parallel_mixer(ph):
                i = ph.i
                act.wait_ge(S["decay_x"], i + 1)
                l = m2_la[:, 1]
                chain(A_(l, m2_la[:, 0], ACT.Abs))
                chain(A_(l, l, ACT.Exp, scale=-1.0))
                A_(l, l, ACT.Ln, bias=1.0).then_inc(S["decay_l"], 1)
                for t in range(TT):
                    act.wait_ge(S["diag_in"], 2 * i + t + 1)
                    d = m2_diag[:, t].rearrange("p a b c -> p (a b c)")
                    A_(d, d, ACT.Exp).then_inc(S["diag_exp"], 1)
                act.wait_ge(S["qs_in"], i + 1)
                A_(m2_la[:, 2], m2_la[:, 2], ACT.Exp).then_inc(S["qs_exp"], 1)
                for n in range(1, 2 * NSUB):
                    m = 15 * i + n
                    act.wait_ge(S["ks_in"], seen(m))
                    w = P if n <= NSUB else TOK
                    k = m2_ks[:, m % 4, 0:w]
                    A_(k, k, ACT.Exp, scale=-1.0).then_inc(S["ks_exp"], 1)
                act.wait_ge(S["wide_read"], ph.at["wide_read"] + 14)
                A_(m2_tmp[:, 0].rearrange("p (t n) -> p t n", t=TT), m2_gv[:, :, 256:512],
                   ACT.Silu).then_inc(S["out_gate"], 1)
                move_turned(act, ph, range(4), move, "moved_even")
                for u in range(2 * DA_HEADS + 1):
                    if u < 2 * DA_HEADS:
                        act.wait_ge(S["probs_T"], seen(ph.at.get("probs_T", 0) + u // 2))
                        soft_exp(ph, u)
                    if u >= 2 and u % 2 == 0:
                        move_probs(ph, u // 2 - 1)
                move_turned(act, ph, range(4, 8), move, "moved_even")

            def product_keys(ph):
                act.wait_ge(S["normed"], ph.at["normed"])
                act.dma_start(pk_keys[:, 0], A["peer_keys1_2"][ph.i]).then_inc(S["keys_in"], 16)
                act.dma_start(pk_keys[:, 1], A["peer_keys2_2"][ph.i]).then_inc(S["keys_in"], 16)
                move_turned(act, ph, range(2), move, "moved_even")
                for n in range(8):
                    act.wait_ge(S["key_scores"], seen(8 * ph.i + n + 1))
                    t, g = n // 4, n % 4
                    A_(pk_S[:, t, 4 * g:4 * g + 4].rearrange("p c n -> p (c n)"), work[n % 4][:, :],
                       ACT.Copy).then_inc(S["key_scores_read"], 1)
                for t in range(TT):
                    act.wait_ge(S["gate_exp_in"], seen(2 * ph.i + t + 1))
                    g = pk_gate[:, t]
                    A_(g, g, ACT.Exp).then_inc(S["gate_exp"], 1)
                for t in range(TT):
                    act.wait_ge(S["dots_moved"], seen(16 * (2 * ph.i + t) + 8))
                    act.wait_ge(S["row_used"], ph.at.get("row_used", 0) + 256 * t)
                    A_(pk_coef, pk_dot, ACT.Gelu).then_inc(S["gelu"], 1)

            act.wait_ge(S["trig_in"], 1)
            A_(trig[:].rearrange("p a t f -> p (a t f)"),
               ang[:, 2:4].rearrange("p a t f -> p (a t f)"), ACT.Sin).then_inc(S["trig"], 1)
            act.wait_ge(S["lam_in"], 1)
            A_(small[:, 24:28], small[:, 20:24], ACT.Exp).then_inc(S["lam_exp"], 1)
            for ph in phases:
                {"norm": norm, "norm_ffn": norm, "norm_final": norm, "ffn": ffn, "sb": stick_breaking,
                 "moba": block_attention, "mla": latent_attention, "mix2": parallel_mixer,
                 "peer": product_keys}[ph.kind](ph)

        @block.vector
        def _(dve):
            V = nc.vector
            chain = Chain(dve, "dve_chain")

            def move(dst, src):
                return V.tensor_copy(dst, src)

            def take_wide(ph):
                for k, (_, _, _, c0, n, layout) in enumerate(panels(ph)):
                    if ph.kind == "mla" and k == 2:
                        latent_norms(ph)
                    for j in range(2):
                        t = ph.at["wide"] + 2 * k + j
                        dve.wait_ge(S["wide"], t + 1)
                        b = work[t % 4]
                        if ph.kind == "sb":
                            if layout == "T":
                                dst = (sb_qT if k < 2 else sb_kT)[:, 4 * (k % 2) + 2 * j:
                                                                  4 * (k % 2) + 2 * j + 2]
                                dst = dst.rearrange("p c t -> p (c t)")
                            else:
                                dst = sb_v[:, j, (k - 4) * 512:(k - 3) * 512]
                        elif ph.kind == "moba":
                            dst = (mo_qk[:, j, k * 512:(k + 1) * 512] if k < 4 else
                                   mo_v[:, j, (k - 4) * 512:(k - 3) * 512])
                        elif ph.kind == "mla":
                            if k < 2:
                                dst = ml_c[:, j, c0:c0 + n]
                            elif k < 5:
                                dst = ml_q[:, j].rearrange("p h d -> p (h d)")[:, (k - 2) * 512:(k - 1) * 512]
                            else:
                                h0 = 4 * (k - 5)
                                s = b[:, :].rearrange("p (h x) -> p h x", h=4)
                                V.tensor_copy(ml_k[:, j, h0:h0 + 4, 0:64], s[:, :, 0:64])
                                V.tensor_copy(ml_v[:, j, h0 * 64:(h0 + 4) * 64].rearrange(
                                    "p (h x) -> p h x", h=4), s[:, :, 64:128]).then_inc(S["wide_read"], 1)
                                continue
                        elif ph.kind == "mix2":
                            if k < 2:
                                dst = m2_qk[:, j, k * 512:(k + 1) * 512]
                            elif k == 2:
                                dst = m2_v[:, j]
                            elif k == 3 or (k == 4 and j == 0):
                                c = 4 * (k - 3) + 2 * j
                                dst = m2_sc[:, c:c + 2].rearrange("p c t -> p (c t)")
                            elif k == 4:
                                dst = m2_gq.rearrange("p c t -> p (c t)")
                            elif k == 5:
                                dst = m2_gv[:, j]
                            else:
                                V.tensor_copy(m2_lr[0:GLA_RANK, j * P:(j + 1) * P],
                                              b[0:GLA_RANK, 0:P]).then_inc(S["wide_read"], 1)
                                continue
                        else:
                            c = 4 * k + 2 * j
                            dst = pk_qT[:, c:c + 2].rearrange("p c t -> p (c t)")
                        V.tensor_copy(dst, b[:, 0:n]).then_inc(S["wide_read"], 1)

            def norm(ph):
                at = ph.at
                gslot = at.get("gains", 0) % 2
                dve.wait_ge(S["square_sum"], at.get("square_sum", 0) + 2)
                V.tensor_scalar(small[:, 2:4], small[:, 0:2], 1.0 / D, EPS, ALU.mult,
                                ALU.add).then_inc(S["mean_square"], 1)
                dve.wait_ge(S["rstd"], at.get("rstd", 0) + 1)
                dve.wait_ge(gain_in[gslot], 16 * (at.get("gains", 0) // 2 + 1))
                to_resid = ph.kind == "norm_final" and not ph.last
                for t in range(TT):
                    V.scalar_tensor_tensor(out=(resid if to_resid else xn)[:, t], in0=resid[:, t],
                                           scalar=small[:, 4 + t:5 + t], in1=gains[:, gslot],
                                           op0=ALU.mult, op1=ALU.mult).then_inc(S["normed"], 1)
                if ph.kind == "norm":
                    move_turned(dve, ph, range(4), move, "moved_odd")
                elif ph.kind == "norm_ffn":
                    for g in range(4):
                        n = at.get("turned", 0) + g
                        dve.wait_ge(S["x_hi"], at.get("x_hi", 0) + g + 1)
                        t, half = g // 2, g % 2
                        hi, lo = (x[:, 4 * half:4 * half + 4, t * P:(t + 1) * P] for x in (x_hi, x_lo))
                        V.tensor_tensor(lo, work[n % 4][:, :].rearrange("p (a b) -> p a b", a=4),
                                        hi.bitcast(F32), ALU.subtract
                                        ).then_inc(S["moved_odd" if n % 2 else "moved_even"], 1)

            def add_deep(ph, n, scale):
                dve.wait_ge(S["deep"], ph.at.get("deep", 0) + n)
                for t in range(TT):
                    for h in range(2):
                        r = resid[:, t, h * 512:(h + 1) * 512]
                        V.scalar_tensor_tensor(out=r, in0=acc[t][h][:, :], scalar=scale, in1=r,
                                               op0=ALU.mult, op1=ALU.add).then_inc(S["resid"], 1)

            def ffn(ph):
                at = ph.at

                def gated(s, j, r=None):
                    n = at.get("wide", 0) + 2 * s + j
                    silus, d = at.get("silu", 0) + 2 * s + j + 1, at.get("deep", 0) + s - 1
                    if r is None:
                        dve.wait_ge(S["silu"], silus)
                        dve.wait_ge(S["deep"], seen(d))
                    else:
                        dve.wait_ge(S["silu"], r * 8 + silus)
                        dve.wait_ge(S["deep"], r * 4 + d)
                    V.tensor_tensor(hidden[:, n % 2], work[n % 4][:, TOK:2 * TOK], silu_buf[:, n % 2],
                                    ALU.mult).then_inc(S["gated"], 1)
                    need = at.get("gated", 0) + 2 * s + j + 1
                    dve.wait_ge(S["gated"], need if r is None else r * 8 + need)
                    V.tensor_copy(hid_hi[:, n % 4], hidden[:, n % 2]).then_inc(S["hid_hi"], 1)

                def gated_rest(s, j, r=None):
                    n = at.get("wide", 0) + 2 * s + j
                    need = at.get("hid_hi", 0) + 2 * s + j + 1
                    dve.wait_ge(S["hid_hi"], need if r is None else r * 8 + need)
                    V.tensor_tensor(hid_lo[:, n % 4], hidden[:, n % 2], hid_hi[:, n % 4].bitcast(F32),
                                    ALU.subtract).then_inc(S["wide_read"], 1)

                def wide_half(s, j, r=None):
                    need = at.get("wide_hi", 0) + 2 * s + j + 1
                    dve.wait_ge(S["wide_hi"], need if r is None else r * 8 + need)
                    slot = (at.get("wide", 0) // 2 + s) % GSLOTS
                    V.tensor_tensor(wide_lo[:, j], halves(wide_ring[:, slot])[j],
                                    wide_hi[:, j].bitcast(F32), ALU.subtract
                                    ).then_inc(S["wide_lo"], 1)

                def deep_panel(s, r=None):
                    need = at.get("deep_hi", 0) + s + 1
                    dve.wait_ge(S["deep_hi"], need if r is None else r * 4 + need)
                    slot = (at.get("deep", 0) + s) % DSLOTS
                    V.tensor_tensor(deep_lo[:], deep_ring[:, slot], deep_hi[:].bitcast(F32),
                                    ALU.subtract).then_inc(S["deep_lo"], 1)

                def step(s, r=None):
                    for j in range(2):
                        gated(s - 1, j, r)
                        wide_half(s, j, r)
                        gated_rest(s - 1, j, r)
                    deep_panel(s - 1, r)
                wide_half(0, 0)
                wide_half(0, 1)
                step(1)
                step(2)
                with dve.Fori(0, 2) as r:
                    for s in range(3, 7):
                        step(s, r)
                for j in range(2):
                    gated(FFN_STEPS - 1, j)
                    gated_rest(FFN_STEPS - 1, j)
                deep_panel(FFN_STEPS - 1)
                add_deep(ph, FFN_STEPS, 0.5)

            def mixed_out(ph, h, o):
                dve.wait_ge(S["mixed"], ph.at.get("mixed", 0) + h + 1)
                p0 = HD * (h % 2)
                V.tensor_copy(o[p0:p0 + HD, h // 2], work[3][p0:p0 + HD, (h % 2) * TOK:(h % 2 + 1) * TOK]
                              ).then_inc(S["mixed_read"], 1)

            def stick_breaking(ph):
                at = ph.at
                take_wide(ph)
                for i in range(HEADS + 2):
                    if i < HEADS:
                        dve.wait_ge(S["scores"], at.get("scores", 0) + i + 1)
                        dve.wait_ge(S["tail_read"], seen(at.get("tail_read", 0) + i - 1))
                        V.scalar_tensor_tensor(out=core_a[:, i % 2], in0=work[i % 2][:, 0:TRI],
                                               scalar=HD ** -0.5, in1=mask_T[:], op0=ALU.mult,
                                               op1=ALU.add).then_inc(S["masked"], 1)
                    if 0 <= i - 1 < HEADS:
                        h = i - 1
                        dve.wait_ge(S["tail"], at.get("tail", 0) + h + 1)
                        dve.wait_ge(S["weights"], seen(at.get("weights", 0) + h - 1))
                        V.tensor_tensor(core_d[:, h % 2], core_a[:, h % 2], work[2][:, 0:TRI],
                                        ALU.subtract).then_inc(S["tail_read"], 1)
                    if 0 <= i - 2 < HEADS:
                        mixed_out(ph, i - 2, oT)
                    if i < HEADS:
                        dve.wait_ge(S["log1p"], at.get("log1p", 0) + i + 1)
                        dve.wait_ge(S["tail"], seen(at.get("tail", 0) + i - 1))
                        V.scalar_tensor_tensor(out=core_c[:, i % 2], in0=core_a[:, i % 2], scalar=0.0,
                                               in1=core_b[:, i % 2], op0=ALU.max,
                                               op1=ALU.add).then_inc(S["softplus"], 1)
                add_deep(ph, 4, 1.0)

            def soft_mask(ph, u, scale):
                dve.wait_ge(S["scores"], ph.at.get("scores", 0) + u + 1)
                dve.wait_ge(S["exps"], seen(ph.at.get("exps", 0) + u - 1))
                V.scalar_tensor_tensor(out=core_a[:, u % 2], in0=work[u % 2][:, 0:TRI], scalar=scale,
                                       in1=mask_rows[:], op0=ALU.mult, op1=ALU.add
                                       ).then_inc(S["masked"], 1)
                dve.wait_ge(S["masked"], ph.at.get("masked", 0) + u + 1)
                m = 8 + 2 * (u % 2)
                V.tensor_reduce(small[:, m:m + 1], core_a[:, u % 2, 0:P], AX, ALU.max, negate=True)
                V.tensor_reduce(small[:, m + 1:m + 2], core_a[:, u % 2, P:TRI], AX, ALU.max,
                                negate=True).then_inc(S["row_max"], 1)

            def soft_norm(ph, u):
                dve.wait_ge(S["exps"], ph.at.get("exps", 0) + u + 1)
                m = 2 * (u % 2)
                chain(V.reciprocal(small[:, 16 + m:18 + m], small[:, 12 + m:14 + m]))
                e = core_b[:, u % 2]
                V.tensor_scalar(e[:, 0:P], e[:, 0:P], small[:, 16 + m:17 + m], None, ALU.mult)
                V.tensor_scalar(e[:, P:TRI], e[:, P:TRI], small[:, 17 + m:18 + m], None,
                                ALU.mult).then_inc(S["probs"], 1)

            def softmax_heads(ph, scale, o):
                for i in range(HEADS + 2):
                    if i < HEADS:
                        soft_mask(ph, i, scale)
                    if 0 <= i - 1 < HEADS:
                        soft_norm(ph, i - 1)
                    if 0 <= i - 2 < HEADS:
                        mixed_out(ph, i - 2, o)
                add_deep(ph, 4, 1.0)

            def rotate(x, t, f, at, tmp):
                heads = x.shape[1]
                a, b = x[:, :, 0:f], x[:, :, f:2 * f]
                cos = trig[:, 0, t, at:at + f].unsqueeze(1).to_broadcast([P, heads, f])
                sin = trig[:, 1, t, at:at + f].unsqueeze(1).to_broadcast([P, heads, f])
                tm = [tmp[:, i * heads * f:(i + 1) * heads * f].rearrange("p (h f) -> p h f", f=f)
                      for i in range(4)]
                V.tensor_tensor(tm[0], a, cos, ALU.mult)
                V.tensor_tensor(tm[1], b, sin, ALU.mult)
                V.tensor_tensor(tm[2], a, sin, ALU.mult)
                chain(V.tensor_tensor(tm[3], b, cos, ALU.mult))
                V.tensor_tensor(a, tm[0], tm[1], ALU.subtract)
                return V.tensor_tensor(b, tm[2], tm[3], ALU.add)

            def block_attention(ph):
                take_wide(ph)
                dve.wait_ge(S["wide_read"], ph.at["wide_read"] + 12)
                for t in range(TT):
                    x = mo_qk[:, t].rearrange("p (h d) -> p h d", d=HD)[:, :, 0:16]
                    ins = rotate(x, t, 8, FREQ_AT[0], mo_tmp)
                    if t == 0:
                        chain(ins)
                ins.then_inc(S["rotated"], 1)
                move_turned(dve, ph, range(8), move, "moved_odd")
                softmax_heads(ph, HD ** -0.5, oT)

            def rms_scales(ph, k, n, width, name_at):
                V.tensor_scalar(small[:, 48:48 + n], small[:, 32:32 + n], 1.0 / width, EPS, ALU.mult,
                                ALU.add).then_inc(S["mean_square"], 1)

            def latent_norms(ph):
                dve.wait_ge(S["wide_read"], ph.at["wide_read"] + 4)
                spans = [(0, Q_RANK), (Q_RANK, Q_RANK + KV_RANK)]
                for t in range(TT):
                    for s, (a, b) in enumerate(spans):
                        chain(V.tensor_tensor_reduce(
                            out=ml_k[:, 0].rearrange("p h d -> p (h d)")[:, 0:b - a],
                            in0=ml_c[:, t, a:b], in1=ml_c[:, t, a:b], scale=1.0 / (b - a), scalar=0.0,
                            op0=ALU.mult, op1=ALU.add, accum_out=small[:, 32 + 2 * t + s:33 + 2 * t + s]))
                V.tensor_scalar(small[:, 48:52], small[:, 32:36], EPS, None,
                                ALU.add).then_inc(S["mean_square"], 1)
                dve.wait_ge(S["rstd"], ph.at["rstd"] + 1)
                for t in range(TT):
                    for s, (a, b) in enumerate(spans):
                        V.scalar_tensor_tensor(out=ml_c[:, t, a:b], in0=ml_c[:, t, a:b],
                                               scalar=small[:, 52 + 2 * t + s:53 + 2 * t + s],
                                               in1=mla_gain[:, a:b], op0=ALU.mult, op1=ALU.mult)
                    r = ml_c[:, t, Q_RANK + KV_RANK:].unsqueeze(1)
                    chain(rotate(r, t, 16, FREQ_AT[1], ml_k[:, 1, 0:4].rearrange("p h d -> p (h d)")))
                V.tensor_copy(small[:, 60:61], small[:, 52:53]).then_inc(S["rotated"], 1)
                move_turned(dve, ph, range(4), move, "moved_odd")

            def latent_attention(ph):
                take_wide(ph)
                dve.wait_ge(S["wide_read"], ph.at["wide_read"] + 18)
                for t in range(TT):
                    r = ml_c[:, t, Q_RANK + KV_RANK:].unsqueeze(1).to_broadcast([P, HEADS, ROPE])
                    ins = V.tensor_copy(ml_k[:, t, :, 64:MLA_QK], r)
                ins.then_inc(S["rotated"], 1)
                for t in range(TT):
                    ins = rotate(ml_q[:, t, :, 64:MLA_QK], t, 16, FREQ_AT[1], ml_T[:, 0:2].rearrange(
                        "p a b -> p (a b)"))
                    if t == 0:
                        chain(ins)
                ins.then_inc(S["rotated"], 1)
                move_turned(dve, ph, range(4, 20), move, "moved_odd")
                softmax_heads(ph, MLA_QK ** -0.5, ml_oT)

            def parallel_mixer(ph):
                i, at = ph.i, ph.at
                take_wide(ph)
                dve.wait_ge(S["wide_read"], at["wide_read"] + 14)
                for c in range(2):
                    z = m2_sc[:, 2 + c]
                    y = m2_mixT[:, 4 + c]
                    chain(V.tensor_tensor(z, z, m2_sc[:, 4 + c], ALU.mult))
                    w = conv_taps[:, i, c]
                    chain(V.tensor_scalar(y, z, w[:, 2:3], None, ALU.mult))
                    for j in (1, 0):
                        s = 2 - j
                        chain(V.scalar_tensor_tensor(out=y[:, s:], in0=z[:, 0:TOK - s],
                                                     scalar=w[:, j:j + 1], in1=y[:, s:],
                                                     op0=ALU.mult, op1=ALU.add))
                    ins = V.tensor_tensor(y, y, m2_sc[:, c], ALU.mult)
                ins.then_inc(S["conv_done"], 1)
                dve.wait_ge(S["gate_mm"], i + 1)
                V.tensor_scalar(m2_la[:, 0], work[0][:, 0:TOK], gate_bias[:, i:i + 1], None,
                                ALU.add).then_inc(S["decay_x"], 1)
                dve.wait_ge(S["decay_l"], i + 1)
                chain(V.scalar_tensor_tensor(out=m2_la[:, 0], in0=m2_la[:, 0], scalar=0.0,
                                             in1=m2_la[:, 1], op0=ALU.min, op1=ALU.subtract))
                chain(V.tensor_scalar(m2_la[:, 0], m2_la[:, 0], 1.0 / GLA_TEMP, None, ALU.mult))
                chain(V.tensor_tensor_scan(m2_b, m2_la[:, 0], zeros_tok[:], 0.0, ALU.add, ALU.add))
                b = m2_b
                q, k = m2_gq[:, 0], m2_gq[:, 1]
                chain(V.tensor_scalar(q, q, GLA_DK ** -0.5, None, ALU.mult))
                full = [P, SUB, NSUB, SUB]

                def by_i(v, t):
                    return v[:, t * P:(t + 1) * P].rearrange("p (n i) -> p i n", i=SUB).unsqueeze(
                        3).to_broadcast(full)

                def by_j(v, t):
                    return v[:, t * P:(t + 1) * P].rearrange("p (n j) -> p n j", j=SUB).unsqueeze(
                        1).to_broadcast(full)
                for t in range(TT):
                    d = m2_diag[:, t]
                    chain(V.tensor_tensor(d, by_i(b, t), by_j(b, t), ALU.subtract))
                    V.tensor_scalar(d, d, 0.0, None, ALU.min).then_inc(S["diag_in"], 1)
                e = m2_la[:, 2]
                chain(V.tensor_copy(e[:, 0:SUB], b[:, 0:SUB]))
                V.tensor_tensor(e[:, SUB:].rearrange("p (n i) -> p n i", i=SUB),
                                b[:, SUB:].rearrange("p (n i) -> p n i", i=SUB),
                                b[:, SUB - 1:TOK - SUB:SUB].unsqueeze(2).to_broadcast(
                                    [P, 2 * NSUB - 1, SUB]), ALU.subtract).then_inc(S["qs_in"], 1)
                for t in range(TT):
                    dve.wait_ge(S["diag_exp"], 2 * i + t + 1)
                    d = m2_diag[:, t]
                    chain(V.tensor_tensor(d, d, by_i(q, t), ALU.mult))
                    V.tensor_tensor(d, d, by_j(k, t), ALU.mult).then_inc(S["diag_ready"], 1)
                dve.wait_ge(S["qs_exp"], i + 1)
                chain(V.tensor_tensor(e, e, q, ALU.mult))
                for h in range(GLA_HEADS):
                    ins = V.tensor_scalar(m2_qsb[:, :, h, :], e.rearrange("p (n i) -> p n i", i=SUB),
                                          head_of[:, h:h + 1], None, ALU.mult)
                ins.then_inc(S["qs_ready"], 1)
                for n in range(1, 2 * NSUB + 2):
                    m = 15 * i + n
                    w = P if n <= NSUB else TOK
                    if n < 2 * NSUB:
                        dve.wait_ge(S["off_mm"], seen(m - 4))
                        V.tensor_scalar(m2_ks[:, m % 4, 0:w], b[:, 0:w], b[:, SUB * n - 1:SUB * n], 0.0,
                                        ALU.subtract, ALU.max).then_inc(S["ks_in"], 1)
                    if n >= 3:
                        m, w = m - 2, P if n - 2 <= NSUB else TOK
                        dve.wait_ge(S["ks_exp"], seen(m))
                        V.tensor_tensor(m2_ks[:, m % 4, 0:w], m2_ks[:, m % 4, 0:w], k[:, 0:w],
                                        ALU.mult).then_inc(S["ks_ready"], 1)
                dve.wait_ge(S["diag_mm"], seen(2 * (i + 1)))
                dve.wait_ge(S["off_mm"], seen(15 * (i + 1)))
                early = earlier_sub[:].unsqueeze(1).unsqueeze(3).to_broadcast([P, GLA_HEADS, NSUB, SUB])
                for blk, src in ((0, work[2]), (2, bank[0])):
                    dst = m2_AT[:, blk].rearrange("p h (n i) -> p h n i", i=SUB)
                    a = src[:, :].rearrange("p (n h i) -> p h n i", h=GLA_HEADS, i=SUB)
                    V.memset(dst[:, :, 0:1], 0.0)
                    V.tensor_tensor(dst[:, :, 1:], a[:, :, 1:], early[:, :, 1:], ALU.mult)
                chain(V.tensor_copy(m2_AT[:, 1].rearrange("p h (n i) -> p h n i", i=SUB),
                                    work[3][:, :].rearrange("p (n h i) -> p h n i", h=GLA_HEADS, i=SUB)))
                for t in range(TT):
                    g = work[1][:, t * 64:(t + 1) * 64].rearrange("p (i h) -> p h i", h=GLA_HEADS)
                    for h in range(GLA_HEADS):
                        gh = g[:, h].unsqueeze(1).to_broadcast([P, NSUB, SUB])
                        tmp = m2_tmp[:, 1, 0:P].rearrange("p (n i) -> p n i", i=SUB)
                        chain(V.tensor_tensor(tmp, gh, same_sub[:], ALU.mult))
                        a = m2_AT[:, 2 * t, h].rearrange("p (n i) -> p n i", i=SUB)
                        ins = V.tensor_tensor(a, a, tmp, ALU.add)
                        if (t, h) != (1, GLA_HEADS - 1):
                            chain(ins)
                ins.then_inc(S["att_ready"], 1)
                dve.wait_ge(S["gla_mm"], i + 1)
                og = m2_og.rearrange("p t n -> p (t n)")
                o4 = og.rearrange("p (g e) -> p g e", e=GLA_DV)
                t1 = m2_tmp[:, 1]
                chain(V.tensor_copy(og, bank[1][:, :]))
                chain(V.tensor_tensor(t1, og, og, ALU.mult))
                chain(V.tensor_reduce(small[:, 32:40], t1.rearrange("p (g e) -> p g e", e=GLA_DV), AX,
                                      ALU.add))
                V.tensor_scalar(small[:, 40:48], small[:, 32:40], 1.0 / GLA_DV, EPS, ALU.mult,
                                ALU.add).then_inc(S["mean_square"], 1)
                dve.wait_ge(S["rstd"], at["rstd"] + 1)
                chain(V.tensor_tensor(o4, o4, small[:, 48:56].unsqueeze(2).to_broadcast([P, 8, GLA_DV]),
                                      ALU.mult))
                chain(V.tensor_tensor(o4, o4, gla_gain[:, i].unsqueeze(1).to_broadcast([P, 8, GLA_DV]),
                                      ALU.mult))
                dve.wait_ge(S["out_gate"], i + 1)
                chain(V.tensor_tensor(og, og, m2_tmp[:, 0], ALU.mult))
                for t in range(TT):
                    x = m2_qk[:, t].rearrange("p (h d) -> p h d", d=64)[:, :, 0:16]
                    ins = rotate(x, t, 8, FREQ_AT[2], m2_tmp.rearrange("p a b -> p (a b)"))
                    if t == 0:
                        chain(ins)
                ins.then_inc(S["rotated"], 1)
                move_turned(dve, ph, range(4), move, "moved_odd")
                for u in range(2 * DA_HEADS + 3):
                    if u < 2 * DA_HEADS:
                        soft_mask(ph, u, 64 ** -0.5)
                    if 1 <= u <= 2 * DA_HEADS:
                        n = u - 1
                        if n % 2 == 0:
                            soft_norm(ph, n)
                        else:
                            dve.wait_ge(S["exps"], at.get("exps", 0) + n + 1)
                            chain(V.reciprocal(small[:, 18:20], small[:, 14:16]))
                            chain(V.tensor_scalar(small[:, 18:20], small[:, 18:20],
                                                  minus_lam[:, i:i + 1], None, ALU.mult))
                            e1, p0 = core_b[:, 1], core_b[:, 0]
                            V.scalar_tensor_tensor(out=e1[:, 0:P], in0=e1[:, 0:P], scalar=small[:, 18:19],
                                                   in1=p0[:, 0:P], op0=ALU.mult, op1=ALU.add)
                            V.scalar_tensor_tensor(out=e1[:, P:], in0=e1[:, P:], scalar=small[:, 19:20],
                                                   in1=p0[:, P:], op0=ALU.mult,
                                                   op1=ALU.add).then_inc(S["probs"], 1)
                    if u >= 4 and u % 2 == 0:
                        h = u // 2 - 2
                        dve.wait_ge(S["mixed"], at.get("mixed", 0) + h + 1)
                        V.tensor_copy(m2_od[:, :, h * DA_V:(h + 1) * DA_V],
                                      work[3][:, (h % 2) * 256:(h % 2) * 256 + 256].rearrange(
                                          "p (t e) -> p t e", t=TT)).then_inc(S["mixed_read"], 1)
                dve.wait_ge(S["mixed"], at.get("mixed", 0) + DA_HEADS)
                od = m2_od.rearrange("p t n -> p (t n)")
                o8 = od.rearrange("p (g e) -> p g e", e=DA_V)
                sq = m2_tmp.rearrange("p a b -> p (a b)")
                dve.wait_ge(S["mixed_read"], at.get("mixed_read", 0) + DA_HEADS)
                chain(V.tensor_tensor(sq, od, od, ALU.mult))
                chain(V.tensor_reduce(small[:, 32:40], sq.rearrange("p (g e) -> p g e", e=DA_V), AX,
                                      ALU.add))
                V.tensor_scalar(small[:, 40:48], small[:, 32:40], 1.0 / DA_V, EPS, ALU.mult,
                                ALU.add).then_inc(S["mean_square"], 1)
                dve.wait_ge(S["rstd"], at["rstd"] + 2)
                keep = 1.0 - (0.8 - 0.6 * math.exp(-0.3 * i))
                chain(V.tensor_scalar(small[:, 48:56], small[:, 48:56], keep, None, ALU.mult))
                chain(V.tensor_tensor(o8, o8, small[:, 48:56].unsqueeze(2).to_broadcast([P, 8, DA_V]),
                                      ALU.mult))
                V.tensor_tensor(o8, o8, diff_gain[:, i].unsqueeze(1).to_broadcast([P, 8, DA_V]),
                                ALU.mult).then_inc(S["rotated"], 1)
                move_turned(dve, ph, range(4, 8), move, "moved_odd")
                add_deep(ph, 4, 1.0)

            def top16(vals, idx, src):
                chain(V.max(vals[:, 0:8], src))
                V.max_index(idx[:, 0:8], vals[:, 0:8], src)
                chain(V.match_replace(src, vals[:, 0:8], src, -3e38))
                chain(V.max(vals[:, 8:16], src))
                chain(V.max_index(idx[:, 8:16], vals[:, 8:16], src))

            def pick(ph, t):
                dve.wait_ge(S["key_scores_read"], seen(8 * ph.i + 4 * (t + 1)))
                for c in range(16):
                    top16(pk_v[:, c], pk_i[:, c], pk_S[:, t, c])
                for h in range(PK_HEADS):
                    v1, v2 = pk_v[:, 2 * h], pk_v[:, 2 * h + 1]
                    chain(V.tensor_tensor(pk_cand.rearrange("p (a b) -> p a b", a=TOPK),
                                          v1.unsqueeze(2).to_broadcast([P, TOPK, TOPK]),
                                          v2.unsqueeze(1).to_broadcast([P, TOPK, TOPK]), ALU.add))
                    top16(pk_sc[:, h], pk_ci[:, h], pk_cand)
                g = pk_gate[:, t].rearrange("p (h s) -> p h s", s=TOPK)
                V.tensor_tensor(g, pk_sc, pk_sc[:, :, 0:1].to_broadcast([P, PK_HEADS, TOPK]),
                                ALU.subtract).then_inc(S["gate_exp_in"], 1)
                ci = pk_ci.rearrange("p h s -> p (h s)")
                V.tensor_scalar(pk_abu[:, 0], ci, 4, None, ALU.logical_shift_right)
                V.tensor_scalar(pk_abu[:, 1], ci, 15, None, ALU.bitwise_and)
                chain(V.tensor_copy(pk_if.rearrange("p a b -> p (a b)"),
                                    pk_i.rearrange("p a b -> p (a b)")))
                chain(V.tensor_copy(pk_ab.rearrange("p a b -> p (a b)"),
                                    pk_abu.rearrange("p a b -> p (a b)")))
                shape = [P, PICKS, TOPK]
                for m in range(2):
                    chain(V.tensor_tensor(pk_hot, pk_ab[:, m].unsqueeze(2).to_broadcast(shape),
                                          iota16[:].unsqueeze(1).to_broadcast(shape), ALU.is_equal))
                    hot = pk_hot.rearrange("p (h s) j -> p h s j", h=PK_HEADS)
                    which = pk_if.rearrange("p (h m) j -> p h m j", m=2)[:, :, m].unsqueeze(
                        2).to_broadcast([P, PK_HEADS, TOPK, TOPK])
                    chain(V.tensor_tensor(hot, hot, which, ALU.mult))
                    chain(V.tensor_reduce(pk_e[:, m], pk_hot, AX, ALU.add))
                chain(V.tensor_scalar(pk_e[:, 0], pk_e[:, 0], float(NKEYS), float(ph.i * EXPERTS),
                                      ALU.mult, ALU.add))
                V.tensor_tensor(pk_idx[:, t], pk_e[:, 0], pk_e[:, 1], ALU.add).then_inc(S["picked"], 1)
                dve.wait_ge(S["gate_exp"], seen(2 * ph.i + t + 1))
                chain(V.tensor_reduce(pk_den, g, AX, ALU.add))
                chain(V.reciprocal(pk_den, pk_den))
                chain(V.tensor_tensor(g, g, pk_den.unsqueeze(2).to_broadcast([P, PK_HEADS, TOPK]),
                                      ALU.mult))

            def product_keys(ph):
                take_wide(ph)
                move_turned(dve, ph, range(2), move, "moved_odd")
                for t in range(TT):
                    pick(ph, t)
                used = ph.at.get("row_used", 0)
                for t in range(TT):
                    with dve.Fori(0, PICKS // BURST) as r:
                        for n in range(BURST):
                            base = used + 256 * t
                            dve.wait_ge(row_in[n], r * 16 + (16 * (base // BURST) + 16))
                            V.tensor_tensor_reduce(out=pk_scratch, in0=row_ring[:, n], in1=xn[:, t],
                                                   scale=1.0, scalar=0.0, op0=ALU.mult, op1=ALU.add,
                                                   accum_out=pk_dots[:, 0, n:n + 1]
                                                   ).then_inc(S["row_used"], 1)
                            dve.wait_ge(S["row_used"], r * BURST + (base + n + 1))
                        V.tensor_copy(pk_dot[:, ds(r * BURST, BURST)], pk_dots[:, 0]
                                      ).then_inc(S["dots_moved"], 1)
                        dve.wait_ge(S["dots_moved"], r + (16 * (2 * ph.i + t) + 1))
                    dve.wait_ge(S["gelu"], seen(2 * ph.i + t + 1))
                    chain(V.tensor_tensor(pk_coef, pk_coef, pk_gate[:, t], ALU.mult))
                    with dve.Fori(0, PICKS // BURST) as r:
                        V.tensor_copy(pk_dots[:, 1], pk_coef[:, ds(r * BURST, BURST)]
                                      ).then_inc(S["dots_moved"], 1)
                        dve.wait_ge(S["dots_moved"], r + (16 * (2 * ph.i + t) + 9))
                        for n in range(BURST):
                            base = used + 256 * t + PICKS
                            dve.wait_ge(row_in[n], r * 16 + (16 * (base // BURST) + 16))
                            V.scalar_tensor_tensor(out=resid[:, t], in0=row_ring[:, n],
                                                   scalar=pk_dots[:, 1, n:n + 1], in1=resid[:, t],
                                                   op0=ALU.mult, op1=ALU.add
                                                   ).then_inc(S["row_used"], 1)
                            dve.wait_ge(S["row_used"], r * BURST + (base + n + 1))
            mo_tmp = cut(0, 2048)

            for i, r in enumerate(FREQS):
                for f in range(r // 2):
                    inv = float(np.float32(THETA) ** np.float32(-np.float32(2 * f) / np.float32(r)))
                    V.memset(inv_freq[:, FREQ_AT[i] + f:FREQ_AT[i] + f + 1], inv)
            dve.wait_ge(S["params"], 16 * N_PARAMS)
            chain(V.tensor_copy(posf[:, 1], posi[:]))
            dve.wait_ge(S["consts"], 1)
            for t in range(TT):
                for a, b, src in ((0, FREQ_AT[2], 0), (FREQ_AT[2], NFREQ, 1)):
                    ins = V.tensor_scalar(ang[:, 0, t, a:b], inv_freq[:, a:b], posf[:, src, t:t + 1],
                                          None, ALU.mult)
            chain(ins)
            big = 1.5 * 2.0 ** 23
            a0, a1, cs, sn = (ang[:, k] for k in range(4))
            chain(V.tensor_scalar(a1, a0, float(1 / (2 * math.pi)), big, ALU.mult, ALU.add))
            chain(V.tensor_scalar(a1, a1, big, None, ALU.subtract))
            two_pi = 2 * math.pi
            c1 = 6.28125
            c2 = float(np.float32(math.floor((two_pi - c1) * 2 ** 20) / 2 ** 20))
            c3 = two_pi - c1 - c2
            chain(V.scalar_tensor_tensor(out=sn, in0=a1, scalar=-c1, in1=a0, op0=ALU.mult, op1=ALU.add))
            chain(V.scalar_tensor_tensor(out=sn, in0=a1, scalar=-c2, in1=sn, op0=ALU.mult, op1=ALU.add))
            chain(V.scalar_tensor_tensor(out=sn, in0=a1, scalar=-c3, in1=sn, op0=ALU.mult, op1=ALU.add))
            lim = 3.1415925
            chain(V.tensor_scalar(cs, sn, math.pi / 2, None, ALU.add))
            chain(V.tensor_scalar(a1, cs, lim, -two_pi, ALU.is_gt, ALU.mult))
            chain(V.tensor_tensor(cs, cs, a1, ALU.add))
            chain(V.tensor_scalar(cs, cs, lim, -lim, ALU.min, ALU.max))
            V.tensor_scalar(sn, sn, lim, -lim, ALU.min, ALU.max).then_inc(S["trig_in"], 1)
            for i in range(DEPTH2):
                for m in range(2):
                    ins = V.tensor_tensor_reduce(out=ang[:, 0].rearrange("p t f -> p (t f)"),
                                                 in0=lam_rows[:, i, 2 * m], in1=lam_rows[:, i, 2 * m + 1],
                                                 scale=1.0, scalar=0.0, op0=ALU.mult, op1=ALU.add,
                                                 accum_out=small[:, 20 + 2 * i + m:21 + 2 * i + m])
                    if (i, m) != (1, 1):
                        chain(ins)
            ins.then_inc(S["lam_in"], 1)
            dve.wait_ge(S["lam_exp"], 1)
            for i in range(DEPTH2):
                chain(V.tensor_tensor(minus_lam[:, i:i + 1], small[:, 25 + 2 * i:26 + 2 * i],
                                      small[:, 24 + 2 * i:25 + 2 * i], ALU.subtract))
                chain(V.tensor_scalar(minus_lam[:, i:i + 1], minus_lam[:, i:i + 1],
                                      -(0.8 - 0.6 * math.exp(-0.3 * i)), None, ALU.add))
            dve.wait_ge(S["trig"], 1)
            for ph in phases:
                {"norm": norm, "norm_ffn": norm, "norm_final": norm, "ffn": ffn, "sb": stick_breaking,
                 "moba": block_attention, "mla": latent_attention, "mix2": parallel_mixer,
                 "peer": product_keys}[ph.kind](ph)

        @block.gpsimd
        def _(pool):
            G = nc.gpsimd
            chain = Chain(pool, "pool_chain")

            def load_gain(ph):
                name, i = ph.gain
                g = ph.at.get("gains", 0)
                src = A[name] if i is None else A[name][i]
                pool.dma_start(gains[:, g % 2], src.partition_broadcast(P)).then_inc(gain_in[g % 2], 16)
            norms = [ph for ph in phases if ph.kind in NORMS]
            for ph in norms[:2]:
                load_gain(ph)

            def select(m, pattern, op, fill, base, cm):
                chain(G.affine_select(out=m, in_=m, pattern=pattern, compare_op=op, fill=fill,
                                      base=base, channel_multiplier=cm))
            G.memset(ident[:], 0.0)
            G.memset(later[:], 1.0)
            G.memset(mask_T[:], 0.0)
            G.memset(mask_rows[:], 0.0)
            G.memset(head_of[:], 1.0)
            G.memset(earlier_sub[:], 1.0)
            G.memset(same_sub[:], 1.0)
            G.memset(minus_half[:], -0.5)
            G.memset(zeros_tok[:], 0.0)
            G.iota(iota16[:], pattern=[[1, TOPK]], base=0, channel_multiplier=0,
                   allow_small_or_imprecise_dtypes=True)
            G.iota(posf[:, 0], pattern=[[P, TT]], base=0, channel_multiplier=1,
                   allow_small_or_imprecise_dtypes=True)
            chain(G.memset(ones[:], 1.0))
            select(ident[:], [[-1, P]], ALU.not_equal, 1.0, 0, 1)
            select(later[:], [[-1, P]], ALU.is_ge, 0.0, 0, 1)
            select(mask_T[:, 0:TOK], [[1, TOK]], ALU.is_gt, NEG, 0, -1)
            select(mask_T[:, TOK:], [[1, P]], ALU.is_gt, NEG, 0, -1)
            select(mask_rows[:, 0:P], [[-1, P]], ALU.is_ge, NEG, 0, 1)
            select(mask_rows[:, P:], [[-1, TOK]], ALU.is_ge, NEG, P, 1)
            select(head_of[:], [[-GLA_DK, GLA_HEADS]], ALU.is_ge, 0.0, 0, 1)
            select(head_of[:], [[GLA_DK, GLA_HEADS]], ALU.is_ge, 0.0, GLA_DK - 1, -1)
            select(earlier_sub[:], [[SUB, NSUB]], ALU.is_gt, 0.0, 0, -1)
            select(same_sub[:], [[-SUB, NSUB], [0, SUB]], ALU.is_ge, 0.0, 0, 1)
            G.affine_select(out=same_sub[:], in_=same_sub[:], pattern=[[SUB, NSUB], [1, SUB]],
                            compare_op=ALU.is_ge, fill=0.0, base=0,
                            channel_multiplier=-1).then_inc(S["consts"], 1)

            def power(ph, k, dst, src):
                pool.wait_ge(S["mean_square"], ph.at.get("mean_square", 0) + k + 1)
                G.tensor_tensor(dst, src, minus_half[:, 0:src.shape[1]], ALU.pow).then_inc(S["rstd"], 1)

            def gather(ph):
                used = ph.at.get("row_used", 0)
                tables = [A["peer_u_2"].rearrange("l e d -> (l e) d"),
                          A["peer_v_2"].rearrange("l e d -> (l e) d")]
                pool.wait_ge(S["wide"], ph.at["wide"] + 8)
                for t in range(TT):
                    pool.wait_ge(S["picked"], seen(2 * ph.i + t + 1))
                    for m in range(2):
                        base = used + 256 * t + PICKS * m

                        def burst(r, parity, first):
                            c = r * (2 * BURST) + parity * BURST
                            G.tensor_copy(pk_burst[:, parity], pk_idx[:, t, ds(c, BURST)]
                                          ).then_inc(S["numbers"], 1)
                            k = (base // BURST) + parity + 1
                            pool.wait_ge(S["numbers"], r * 2 + k)
                            for n in range(BURST):
                                if not first:
                                    pool.wait_ge(S["row_used"],
                                                 r * 2 * BURST + (base + parity * BURST + n - BURST + 1))
                                    pool.sem_inc(S["row_asked"])
                                G.indirect_dma_start(
                                    row_ring[:, n], None, tables[m],
                                    bass.IndirectOffsetOnAxis(ap=pk_burst[:, parity, n:n + 1], axis=0)
                                ).then_inc(row_in[n], 16)
                        if base == 0:
                            burst(0, 0, True)
                            burst(0, 1, False)
                            with pool.Fori(1, PICKS // BURST // 2) as r:
                                for parity in range(2):
                                    burst(r, parity, False)
                        else:
                            with pool.Fori(0, PICKS // BURST // 2) as r:
                                for parity in range(2):
                                    burst(r, parity, False)
            for ph in phases:
                if ph.kind in NORMS:
                    power(ph, 0, small[:, 4:6], small[:, 2:4])
                    k = norms.index(ph)
                    if k >= 1 and k + 1 < len(norms):
                        load_gain(norms[k + 1])
                elif ph.kind == "mla":
                    power(ph, 0, small[:, 52:56], small[:, 48:52])
                elif ph.kind == "mix2":
                    power(ph, 0, small[:, 48:56], small[:, 40:48])
                    power(ph, 1, small[:, 48:56], small[:, 40:48])
                elif ph.kind == "peer":
                    gather(ph)


_INS = ["x", "norm_ffn1", "ffn1_w_gate_up", "ffn1_w_down", "norm_mix", "norm_ffn2", "ffn2_w_gate_up",
        "ffn2_w_down", "sb_w_qkv", "sb_w_o", "moba_w_qkv", "moba_w_o", "mla_w_in", "mla_q_norm",
        "mla_w_uq", "mla_kv_norm", "mla_w_ukv", "mla_w_o", "final_norm", "positions_2", "norm_mix_2",
        "w_in_2", "lam_q1_2", "lam_k1_2", "lam_q2_2", "lam_k2_2", "diff_norm_2", "conv_w_2",
        "gla_w_gate2_2", "gla_b_gate_2", "gla_norm_2", "w_out_2", "norm_ffn_2", "peer_w_q_2",
        "peer_keys1_2", "peer_keys2_2", "peer_u_2", "peer_v_2", "norm_final_2"]
STOP = None


def kernel(**inputs):
    import concourse.bacc as _bacc
    from concourse import mybir as _mybir
    from concourse.bass_utils import run_bass_kernel_spmd as _run

    nc = _bacc.Bacc("TRN2", target_bir_lowering=False, num_devices=1)
    arrays, args = {}, {}
    for name in _INS:
        a = np.ascontiguousarray(inputs[name])
        arrays[f"in_{name}"] = a
        args[name] = nc.dram_tensor(f"in_{name}", a.shape, _mybir.dt.from_np(a.dtype),
                                    kind="ExternalInput").ap()
    out = nc.dram_tensor("out_0", (1, TOK, D), F32, kind="ExternalOutput").ap()
    build(nc, args, out, STOP)
    r = _run(nc, [arrays], core_ids=[0])
    return r.results[0]["out_0"]
```
